# Optimizing a Trainium2 kernel written in Bass

```python
import jax, jax.numpy as jnp
from jax import lax
import numpy as np

D_MODEL = 1024
BATCH = 1
SEQ = 512
DEPTH = 4

CTX_LEN = 256
GRID_W = 64
N_MIXERS = 3
WIDTH = D_MODEL
POOL_WINDOWS = (2, 4, 8, 16)
N_POOL_GROUPS = 4
POOL_GROUP = WIDTH // N_POOL_GROUPS
HEAD_DIM = 64
N_HEADS = WIDTH // HEAD_DIM
WIN_ROWS_MAX = 8
WIN_COLS = 16
CONV_WIDTH = 3
EPS = 1e-6
N_POOL_LAYERS = (DEPTH + 2) // 3
N_NA_LAYERS = (DEPTH + 1) // 3
N_CONV_LAYERS = DEPTH // 3


def _rmsnorm(x, g):
    xf = x.astype(jnp.float32)
    y = xf * lax.rsqrt(jnp.mean(xf * xf, axis=-1, keepdims=True) + EPS)
    return (y * g.astype(jnp.float32)).astype(x.dtype)

def _modulation(cond, w, b):
    m = jax.nn.silu(cond) @ w + b
    return jnp.split(m, 3, axis=-1)

def _centred_mean(u, w):
    b_, l_, c_ = u.shape
    cs = jnp.concatenate([jnp.zeros((b_, 1, c_), jnp.float32),
                          jnp.cumsum(u.astype(jnp.float32), axis=1)], axis=1)
    t = jnp.arange(l_)
    lo = jnp.clip(t - w // 2, 0, l_)
    hi = jnp.clip(t + w // 2, 0, l_)
    cnt = (hi - lo).astype(jnp.float32)
    return ((cs[:, hi] - cs[:, lo]) / cnt[None, :, None]).astype(u.dtype)

def _pool_mixer(h, w_in, w_grp, scale, w_out):
    u, g = jnp.split(h @ w_in, 2, axis=-1)
    b_, l_, _ = u.shape
    ug = u.reshape(b_, l_, N_POOL_GROUPS, POOL_GROUP)
    pooled = jnp.stack([_centred_mean(ug[:, :, i], w) for i, w in enumerate(POOL_WINDOWS)], axis=2)
    mixed = jnp.einsum('blgc,gcd->blgd', pooled - ug, w_grp).reshape(b_, l_, WIDTH)
    return (mixed * scale * jax.nn.silu(g)) @ w_out

def _dwconv3(y, w, b):
    out = lax.conv_general_dilated(y, w[:, None, :], window_strides=(1,), padding=((1, 1),),
                                   dimension_numbers=('NWC', 'WIO', 'NWC'),
                                   feature_group_count=WIDTH)
    return out + b

def _conv_mixer(h, w_in, conv_w, conv_b, w_out):
    bg, cg, v, g = jnp.split(h @ w_in, 4, axis=-1)
    y = bg * _dwconv3(cg * v, conv_w, conv_b)
    return (y * jax.nn.silu(g)) @ w_out

def _na_mixer(h, hc, w_in, rpb, w_out, need_ctx_out):
    b_, l_, _ = h.shape
    rows = l_ // GRID_W
    wr = min(WIN_ROWS_MAX, rows)
    q, k, v, g = jnp.split(h @ w_in, 4, axis=-1)
    q = q.reshape(b_, rows, GRID_W, N_HEADS, HEAD_DIM) * HEAD_DIM ** -0.5
    k = k.reshape(b_, rows, GRID_W, N_HEADS, HEAD_DIM)
    v = v.reshape(b_, rows, GRID_W, N_HEADS, HEAD_DIM)
    if need_ctx_out:
        qc, kc, vc, gc = jnp.split(hc @ w_in, 4, axis=-1)
    else:
        kc, vc = jnp.split(hc @ w_in[:, WIDTH:3 * WIDTH], 2, axis=-1)
    n_ctx = hc.shape[1]
    kc = kc.reshape(b_, n_ctx, N_HEADS, HEAD_DIM)
    vc = vc.reshape(b_, n_ctx, N_HEADS, HEAD_DIM)

    r = jnp.arange(rows)
    row_idx = jnp.clip(r - wr // 2, 0, rows - wr)[:, None] + jnp.arange(wr)[None, :]
    col = jnp.arange(GRID_W)
    col_idx = jnp.clip(col - WIN_COLS // 2, 0, GRID_W - WIN_COLS)[:, None] + jnp.arange(WIN_COLS)[None, :]
    sel = jax.nn.one_hot(col_idx, GRID_W, dtype=h.dtype)

    kb = k[:, row_idx]
    vb = v[:, row_idx]
    s_blk = jnp.einsum('brqhd,brikhd->bhrqik', q, kb)
    s_loc = jnp.einsum('bhrqik,qjk->bhrqij', s_blk, sel).astype(jnp.float32)
    dr_idx = row_idx - r[:, None] + WIN_ROWS_MAX - 1
    dc_idx = col_idx - col[:, None] + WIN_COLS - 1
    bias = rpb[:, dr_idx[:, None, :, None], dc_idx[None, :, None, :]].astype(jnp.float32)
    s_loc = s_loc + bias[None]
    s_ctx = jnp.einsum('brqhd,bchd->bhrqc', q, kc).astype(jnp.float32)
    n_loc = wr * WIN_COLS
    logits = jnp.concatenate([s_loc.reshape(b_, N_HEADS, rows, GRID_W, n_loc), s_ctx], axis=-1)
    p = jax.nn.softmax(logits, axis=-1).astype(v.dtype)
    p_loc = p[..., :n_loc].reshape(b_, N_HEADS, rows, GRID_W, wr, WIN_COLS)
    p_ctx = p[..., n_loc:]
    p_blk = jnp.einsum('bhrqij,qjk->bhrqik', p_loc, sel)
    o = jnp.einsum('bhrqik,brikhd->brqhd', p_blk, vb) + jnp.einsum('bhrqc,bchd->brqhd', p_ctx, vc)
    y = (o.reshape(b_, l_, WIDTH) * jax.nn.silu(g)) @ w_out

    yc = None
    if need_ctx_out:
        qc = qc.reshape(b_, n_ctx, N_HEADS, HEAD_DIM) * HEAD_DIM ** -0.5
        sc = jnp.einsum('bqhd,bkhd->bhqk', qc, kc).astype(jnp.float32)
        pc = jax.nn.softmax(sc, axis=-1).astype(vc.dtype)
        oc = jnp.einsum('bhqk,bkhd->bqhd', pc, vc).reshape(b_, n_ctx, WIDTH)
        yc = (oc * jax.nn.silu(gc)) @ w_out
    return y, yc

def first_inputs(seed: int = 0) -> dict:
    key = jax.random.key(seed)
    ks = jax.random.split(key, 20)
    nrm = jax.random.normal
    d, w = D_MODEL, WIDTH
    return {
        "x": nrm(ks[0], (BATCH, SEQ, d), jnp.float32),
        "c": nrm(ks[1], (BATCH, d), jnp.float32),
        "ctx": nrm(ks[2], (BATCH, CTX_LEN, d), jnp.float32),
        "c_ctx": nrm(ks[3], (d,), jnp.float32),
        "norm_g": 1.0 + 0.02 * nrm(ks[4], (DEPTH, d), jnp.float32),
        "ada_w": 0.5 * d ** -0.5 * nrm(ks[5], (DEPTH, d, 3 * d), jnp.float32),
        "ada_b": 0.01 * nrm(ks[6], (DEPTH, 3 * d), jnp.float32),
        "pool_w_in": d ** -0.5 * nrm(ks[7], (N_POOL_LAYERS, d, 2 * w), jnp.float32),
        "pool_w_grp": POOL_GROUP ** -0.5 * nrm(ks[8], (N_POOL_LAYERS, N_POOL_GROUPS, POOL_GROUP, POOL_GROUP), jnp.float32),
        "pool_scale": 1.0 + 0.1 * nrm(ks[9], (N_POOL_LAYERS, w), jnp.float32),
        "pool_w_out": w ** -0.5 * nrm(ks[10], (N_POOL_LAYERS, w, d), jnp.float32),
        "na_w_in": d ** -0.5 * nrm(ks[11], (N_NA_LAYERS, d, 4 * w), jnp.float32),
        "na_rpb": 0.1 * nrm(ks[12], (N_NA_LAYERS, N_HEADS, 2 * WIN_ROWS_MAX - 1, 2 * WIN_COLS - 1), jnp.float32),
        "na_w_out": w ** -0.5 * nrm(ks[13], (N_NA_LAYERS, w, d), jnp.float32),
        "conv_w_in": d ** -0.5 * nrm(ks[14], (N_CONV_LAYERS, d, 4 * w), jnp.float32),
        "conv_dw": CONV_WIDTH ** -0.5 * nrm(ks[15], (N_CONV_LAYERS, CONV_WIDTH, w), jnp.float32),
        "conv_db": 0.01 * nrm(ks[16], (N_CONV_LAYERS, w), jnp.float32),
        "conv_w_out": w ** -0.5 * nrm(ks[17], (N_CONV_LAYERS, w, d), jnp.float32),
        "final_g": 1.0 + 0.02 * nrm(ks[18], (d,), jnp.float32),
    }

def first_block(x, c, ctx, c_ctx, norm_g, ada_w, ada_b, pool_w_in, pool_w_grp, pool_scale, pool_w_out,
              na_w_in, na_rpb, na_w_out, conv_w_in, conv_dw, conv_db, conv_w_out, final_g):
    last_ctx_reader = max([i for i in range(DEPTH) if i % N_MIXERS == 1], default=-1)
    for i in range(DEPTH):
        kind, j = i % N_MIXERS, i // N_MIXERS
        update_ctx = i < last_ctx_reader
        shift, scale, gate = _modulation(c, ada_w[i], ada_b[i])
        hx = _rmsnorm(x, norm_g[i]) * (1.0 + scale[:, None]) + shift[:, None]
        if kind == 1 or update_ctx:
            cshift, cscale, cgate = _modulation(c_ctx, ada_w[i], ada_b[i])
            hc = _rmsnorm(ctx, norm_g[i]) * (1.0 + cscale) + cshift
        if kind == 0:
            yx = _pool_mixer(hx, pool_w_in[j], pool_w_grp[j], pool_scale[j], pool_w_out[j])
            if update_ctx:
                yc = _pool_mixer(hc, pool_w_in[j], pool_w_grp[j], pool_scale[j], pool_w_out[j])
        elif kind == 1:
            yx, yc = _na_mixer(hx, hc, na_w_in[j], na_rpb[j], na_w_out[j], update_ctx)
        else:
            yx = _conv_mixer(hx, conv_w_in[j], conv_dw[j], conv_db[j], conv_w_out[j])
            if update_ctx:
                yc = _conv_mixer(hc, conv_w_in[j], conv_dw[j], conv_db[j], conv_w_out[j])
        x = x + gate[:, None] * yx
        if update_ctx:
            ctx = ctx + cgate * yc
    return _rmsnorm(x, final_g)


DEPTH_2 = 2

AXIS_DIM = HEAD_DIM // 2
ATTN_WIDTH = D_MODEL // 2
N_Q_HEADS = ATTN_WIDTH // HEAD_DIM
N_KV_HEADS = N_Q_HEADS // 4
KV_WIDTH = N_KV_HEADS * HEAD_DIM
FOURIER_WIDTH = D_MODEL // 4
FOURIER_GROUP = 64
N_FOURIER_GROUPS = FOURIER_WIDTH // FOURIER_GROUP
GMLP_WIDTH = D_MODEL // 4
GMLP_HEAD = 64
N_GMLP_HEADS = GMLP_WIDTH // GMLP_HEAD
CHUNK = 128
Q_BLOCK = 128
MIX_WIDTH = ATTN_WIDTH + FOURIER_WIDTH + GMLP_WIDTH
IN_WIDTH = ATTN_WIDTH + 2 * KV_WIDTH + FOURIER_WIDTH + 2 * GMLP_WIDTH
SPLITS = [ATTN_WIDTH, ATTN_WIDTH + KV_WIDTH, ATTN_WIDTH + 2 * KV_WIDTH,
          ATTN_WIDTH + 2 * KV_WIDTH + FOURIER_WIDTH,
          ATTN_WIDTH + 2 * KV_WIDTH + FOURIER_WIDTH + GMLP_WIDTH]
D_FF = 4 * D_MODEL
ROPE_THETA = 10000.0


def rms_norm(x, g):
    xf = x.astype(jnp.float32)
    y = xf * lax.rsqrt(jnp.mean(xf * xf, axis=-1, keepdims=True) + EPS)
    return (y * g.astype(jnp.float32)).astype(x.dtype)

def modulate(h, shift, scale):
    return h * (1 + scale) + shift

def adaln(cond, w, b):
    return jnp.split(jax.nn.silu(cond) @ w + b, 6, axis=-1)

def axial_rope_tables(n, dtype):
    rows = n // GRID_W
    row = jnp.repeat(jnp.arange(rows, dtype=jnp.float32), GRID_W)
    col = jnp.tile(jnp.arange(GRID_W, dtype=jnp.float32), rows)
    inv = ROPE_THETA ** (-jnp.arange(0, AXIS_DIM, 2, dtype=jnp.float32) / AXIS_DIM)
    ar = (row[:, None] * inv)[:, None, :]
    ac = (col[:, None] * inv)[:, None, :]
    return tuple(t.astype(dtype) for t in (jnp.cos(ar), jnp.sin(ar), jnp.cos(ac), jnp.sin(ac)))

def rope_1d(x, cos, sin):
    x1, x2 = jnp.split(x, 2, axis=-1)
    return jnp.concatenate([x1 * cos - x2 * sin, x1 * sin + x2 * cos], axis=-1)

def apply_axial_rope(x, tabs):
    cr, sr, cc, sc = tabs
    xr, xc = jnp.split(x, 2, axis=-1)
    return jnp.concatenate([rope_1d(xr, cr, sr), rope_1d(xc, cc, sc)], axis=-1)

def heads(t, h):
    return t.reshape(t.shape[0], t.shape[1], h, HEAD_DIM)

def attend(q, k, v):
    s = jnp.einsum('bqkgd,btkd->bkgqt', q, k).astype(jnp.float32) * (HEAD_DIM ** -0.5)
    p = jax.nn.softmax(s, axis=-1).astype(v.dtype)
    return jnp.einsum('bkgqt,btkd->bqkgd', p, v)

def latent_attention(q, k, v):
    b, s, hq, d = q.shape
    g = hq // N_KV_HEADS
    nblk = s // Q_BLOCK
    qb = q.reshape(b, nblk, Q_BLOCK, N_KV_HEADS, g, d).transpose(1, 0, 2, 3, 4, 5)
    out = lax.map(lambda qblk: attend(qblk, k, v), qb)
    return out.transpose(1, 0, 2, 3, 4, 5).reshape(b, s, hq * d)

def context_attention(q, k, v):
    b, n, hq, d = q.shape
    g = hq // N_KV_HEADS
    return attend(q.reshape(b, n, N_KV_HEADS, g, d), k, v).reshape(b, n, hq * d)

def fourier_mix(f):
    b, n, _ = f.shape
    fg = f.astype(jnp.float32).reshape(b, n, N_FOURIER_GROUPS, FOURIER_GROUP)
    y = jnp.fft.fft2(fg, axes=(1, 3), norm='ortho').real
    return y.reshape(b, n, FOURIER_WIDTH).astype(f.dtype)

def chunk_spatial_gate(u, v, v_g, w_s, b_s):
    b, n, _ = u.shape
    u = jax.nn.gelu(u)
    vh = jax.nn.gelu(v).reshape(b, n // CHUNK, CHUNK, N_GMLP_HEADS, GMLP_HEAD)
    vh = rms_norm(vh, v_g.reshape(N_GMLP_HEADS, GMLP_HEAD))
    sp = jnp.einsum('hpq,bcqhd->bcphd', w_s, vh) + b_s.T[None, None, :, :, None]
    return u * sp.reshape(b, n, GMLP_WIDTH)

def squared_relu_mlp(h, w1, w2):
    return jnp.square(jax.nn.relu(h @ w1)) @ w2

def layer(x, ctx, c, c_ctx, w_ada, b_ada, g1, g2, w_in, q_g, k_g, v_g, w_s, b_s, w_out, w1, w2, update_ctx):
    sh1, sc1, gt1, sh2, sc2, gt2 = [m[:, None, :] for m in adaln(c, w_ada, b_ada)]
    csh1, csc1, cgt1, csh2, csc2, cgt2 = adaln(c_ctx, w_ada, b_ada)

    px = modulate(rms_norm(x, g1), sh1, sc1) @ w_in
    pc = modulate(rms_norm(ctx, g1), csh1, csc1) @ w_in
    qx, kx, vx, fx, ux, gvx = jnp.split(px, SPLITS, axis=-1)
    qc, kc, vc, fc, uc, gvc = jnp.split(pc, SPLITS, axis=-1)

    tabs = axial_rope_tables(x.shape[1], x.dtype)
    qx = apply_axial_rope(rms_norm(heads(qx, N_Q_HEADS), q_g), tabs)
    kx = apply_axial_rope(rms_norm(heads(kx, N_KV_HEADS), k_g), tabs)
    kc = rms_norm(heads(kc, N_KV_HEADS), k_g)
    vx = heads(vx, N_KV_HEADS)
    vc = heads(vc, N_KV_HEADS)
    k_all = jnp.concatenate([kc, kx], axis=1)
    v_all = jnp.concatenate([vc, vx], axis=1)

    mix_x = jnp.concatenate([latent_attention(qx, k_all, v_all),
                             fourier_mix(fx),
                             chunk_spatial_gate(ux, gvx, v_g, w_s, b_s)], axis=-1) @ w_out
    x = x + gt1 * mix_x
    x = x + gt2 * squared_relu_mlp(modulate(rms_norm(x, g2), sh2, sc2), w1, w2)

    if update_ctx:
        qc = rms_norm(heads(qc, N_Q_HEADS), q_g)
        mix_c = jnp.concatenate([context_attention(qc, kc, vc),
                                 fourier_mix(fc),
                                 chunk_spatial_gate(uc, gvc, v_g, w_s, b_s)], axis=-1) @ w_out
        ctx = ctx + cgt1 * mix_c
        ctx = ctx + cgt2 * squared_relu_mlp(modulate(rms_norm(ctx, g2), csh2, csc2), w1, w2)
    return x, ctx

def second_inputs(seed: int = 0) -> dict:
    key = jax.random.key(seed)
    ks = jax.random.split(key, 17)
    f32 = jnp.float32
    n = lambda k, s: jax.random.normal(k, s, dtype=f32)
    return {
        'x': n(ks[0], (BATCH, SEQ, D_MODEL)),
        'c': n(ks[1], (BATCH, D_MODEL)),
        'ctx': n(ks[2], (BATCH, CTX_LEN, D_MODEL)),
        'c_ctx': n(ks[3], (D_MODEL,)),
        'w_ada': n(ks[4], (DEPTH_2, D_MODEL, 6 * D_MODEL)) * (0.5 * D_MODEL ** -0.5),
        'b_ada': n(ks[5], (DEPTH_2, 6 * D_MODEL)) * 0.01,
        'norm1_g': 1.0 + 0.02 * n(ks[6], (DEPTH_2, D_MODEL)),
        'norm2_g': 1.0 + 0.02 * n(ks[7], (DEPTH_2, D_MODEL)),
        'w_in': n(ks[8], (DEPTH_2, D_MODEL, IN_WIDTH)) * D_MODEL ** -0.5,
        'q_norm_g': 1.0 + 0.02 * n(ks[9], (DEPTH_2, HEAD_DIM)),
        'k_norm_g': 1.0 + 0.02 * n(ks[10], (DEPTH_2, HEAD_DIM)),
        'gmlp_v_g': 1.0 + 0.02 * n(ks[11], (DEPTH_2, GMLP_WIDTH)),
        'w_spatial': n(ks[12], (DEPTH_2, N_GMLP_HEADS, CHUNK, CHUNK)) * CHUNK ** -0.5,
        'b_spatial': n(ks[13], (DEPTH_2, N_GMLP_HEADS, CHUNK)) * 0.02,
        'w_out': n(ks[14], (DEPTH_2, MIX_WIDTH, D_MODEL)) * MIX_WIDTH ** -0.5,
        'w_mlp1': n(ks[15], (DEPTH_2, D_MODEL, D_FF)) * D_MODEL ** -0.5,
        'w_mlp2': n(ks[16], (DEPTH_2, D_FF, D_MODEL)) * D_FF ** -0.5,
    }

def second_block(x, c, ctx, c_ctx, w_ada, b_ada, norm1_g, norm2_g, w_in, q_norm_g, k_norm_g, gmlp_v_g,
              w_spatial, b_spatial, w_out, w_mlp1, w_mlp2):
    for l in range(DEPTH_2):
        x, ctx = layer(x, ctx, c, c_ctx, w_ada[l], b_ada[l], norm1_g[l], norm2_g[l], w_in[l],
                       q_norm_g[l], k_norm_g[l], gmlp_v_g[l], w_spatial[l], b_spatial[l], w_out[l],
                       w_mlp1[l], w_mlp2[l], l < DEPTH_2 - 1)
    return x


def setup_inputs(seed=0):
    out = dict(first_inputs(seed))
    for name, value in second_inputs(seed + 1).items():
        if name != "x":
            out[name + "_2"] = value
    return out


def reference(
    x, c, ctx, c_ctx, norm_g, ada_w, ada_b, pool_w_in, pool_w_grp, pool_scale, pool_w_out,
    na_w_in, na_rpb, na_w_out, conv_w_in, conv_dw, conv_db, conv_w_out, final_g, c_2, ctx_2,
    c_ctx_2, w_ada_2, b_ada_2, norm1_g_2, norm2_g_2, w_in_2, q_norm_g_2, k_norm_g_2, gmlp_v_g_2,
    w_spatial_2, b_spatial_2, w_out_2, w_mlp1_2, w_mlp2_2,
):
    x = first_block(
        x, c, ctx, c_ctx, norm_g, ada_w, ada_b, pool_w_in, pool_w_grp, pool_scale, pool_w_out,
        na_w_in, na_rpb, na_w_out, conv_w_in, conv_dw, conv_db, conv_w_out, final_g,
    )
    return second_block(
        x, c_2, ctx_2, c_ctx_2, w_ada_2, b_ada_2, norm1_g_2, norm2_g_2, w_in_2, q_norm_g_2,
        k_norm_g_2, gmlp_v_g_2, w_spatial_2, b_spatial_2, w_out_2, w_mlp1_2, w_mlp2_2,
    )


_drawn_inputs = setup_inputs


def setup_inputs(seed=0):
    import zlib

    import numpy as np

    out = dict(_drawn_inputs(seed))
    spreads = {}
    factors = {'ctx': 2.821,
     'norm_g': 4.098,
     'ada_b': 3.607,
     'na_rpb': 8.0,
     'conv_db': 8.0,
     'final_g': 2.781,
     'ctx_2': 5.621,
     'norm1_g_2': 8.0,
     'norm2_g_2': 4.55,
     'q_norm_g_2': 8.0,
     'k_norm_g_2': 8.0,
     'gmlp_v_g_2': 8.0,
     'b_spatial_2': 8.0}
    for name, (base, spread) in spreads.items():
        noise = np.random.default_rng([zlib.crc32(name.encode()), seed]).standard_normal(out[name].shape)
        drawn = base * np.exp(spread * noise) if base else spread * noise
        out[name] = __import__('jax').numpy.asarray(drawn.astype(out[name].dtype))
    for name, factor in factors.items():
        out[name] = (out[name] * factor).astype(out[name].dtype)
    return out
```

```python
from contextlib import ExitStack

import numpy as np
from concourse import mybir

P = 128
D = 1024
KT = D // P
TX, TC = 512, 256
TT = TX + TC
NT = TT // P
EPS = 1e-6
F32 = mybir.dt.float32
F32R = mybir.dt.float32r
ALU = mybir.AluOpType
ACT = mybir.ActivationFunctionType
AX = mybir.AxisListType
GRID_W, ROWS, WIN = 64, 8, 16
NDR = 2 * 8 - 1
NDC = 2 * WIN - 1
NHEADS_NA = 16
PADL = 8
UX, UC = 0, TX + 2 * PADL
UW = TX + TC + 4 * PADL
WINDOWS = (2, 4, 8, 16)
MASKED = -1e30
N_SECT = 24
GELU_C = 0.7978845608028654
GELU_A = 0.044715
SECT0 = [0, 3, 6, 9, 12, 18]
CTX_SECT = {0, 1, 2, 3, 4} | set(range(12, 18)) | {18, 19}


class Step:

    def __init__(self, kind, T=None, m=None, src=None, ev=None, part=None, pair=None, grp=None, layer=None, sect=None,
                 nxT=0, k=None, g=None, c=None, x0=None, what=None, half=None, qt=None, st=None, eb=None, nk=None,
                 first=False, na=False, col=None, tile=None, q0=None, n0=None, nn=None, in_end=None, has_turn=False,
                 after=()):
        self.kind, self.T, self.m, self.src, self.ev, self.part, self.pair = kind, T, m, src, ev, part, pair
        self.grp, self.layer, self.sect, self.nxT, self.k, self.g, self.c = grp, layer, sect, nxT, k, g, c
        self.x0, self.what, self.half, self.qt, self.st, self.eb, self.nk = x0, what, half, qt, st, eb, nk
        self.first, self.na, self.col, self.tile, self.q0, self.n0, self.nn = first, na, col, tile, q0, n0, nn
        self.in_end, self.has_turn, self.after = in_end, has_turn, list(after)
        self.turn, self.w, self.ada = None, None, []


ACT_ONLY, DVE_ONLY = {"u", "v", "cg", "sk", "sq", "sf"}, {"cv", "cb"}


def ends_in(s):
    if s.kind in ("upart", "adastep"):
        return None
    if s.kind in ("bias_row", "gtrans", "four1") or (s.kind == "unit" and s.ev in ACT_ONLY):
        return "act"
    return "dve"


def plan():
    steps = []
    ada_queue = [(s, k) for s in range(N_SECT) for k in range(KT)]
    waiting_red = []

    def add(kind, **a):
        s = Step(kind, **a)
        s.i = len(steps)
        steps.append(s)
        return s

    def with_ada(s, n=1):
        for _ in range(n):
            if ada_queue:
                s.ada.append(ada_queue.pop(0))

    def ada_red(now=False):
        while waiting_red and (now or waiting_red[0][0] < len(steps) - 1):
            add("adared", sect=waiting_red.pop(0)[1], has_turn=True)

    def half_unit(src, ev, T, part, **a):
        return add("unit" if part else "upart", src=src, ev=ev, T=T, m=0, part=part, has_turn=True, **a)

    def full(src, ev, T, m=0, after=(), **a):
        s = add("unit", src=src, ev=ev, T=T, m=m, part=None, has_turn=True, **a)
        s.after = list(after)
        with_ada(s)
        if s.ada and s.ada[-1][1] == KT - 1:
            waiting_red.append((s.i, s.ada[-1][0]))
        ada_red()
        return s

    add("silu_c")
    for k in range(2):
        for c in range(8):
            add("bias_row", g=k, c=c, has_turn=True)
    for s in range(2):
        for k in range(KT):
            x = add("adastep")
            x.ada = [ada_queue.pop(0)]
        add("adared", sect=s, has_turn=True)
    for k in range(KT):
        add("sq0", k=k, T=TT, x0=0)

    def norm(T, g, sect, lx):
        ada_red(True)
        add("nstat", T=T, g=g, sect=sect, has_turn=True)
        return [add("ntile", T=T, k=k, g=g, sect=sect) for k in range(KT)]

    def pool_layer(L, T, nxT):
        tiles = norm(T, L, SECT0[L], L)
        d = []
        for m in range(KT):
            full("H", "u", T, m, after=tiles if m == 0 else ())
            d.append(add("pool", T=T, m=m))
        g = [full("H", "gate", T, m) for m in range(KT)]
        y = []
        for half in range(2):
            for mm in range(4):
                m = half * 4 + mm
                s = add("unit", src="D", ev="poolmix", T=T, m=m, part=None, grp=mm, layer=L // 3, has_turn=True)
                s.after = d[-1:]
                y.append(s)
        for m in range(KT):
            full("H", "xupd", T, m, after=y if m == 0 else (), sect=SECT0[L] + 2, nxT=nxT)

    pool_layer(0, TT, TT)

    tiles = norm(TT, 1, SECT0[1], 1)
    seq = ["q", "k", "g", "v"]
    made = {}
    for j, e in enumerate(seq):
        made[e] = full("H", e, TT if e in "kv" else TX, 0, after=tiles if j == 0 else (), pair=0)
    for t in range(KT):
        vt = add("vtrans")
        vt.after = [made["v"]]
        nxt = {}
        for s in range(8):
            sc = add("scores", na=True, pair=t, half=s // 4, qt=s % 4, st=0, first=(s % 4 == 0), nk=NT)
            sc.after = [made["q"], made["k"]]
            if t + 1 < KT:
                e = seq[s // 2]
                T = TT if e in "kv" else TX
                u = half_unit("H", e, T, s % 2, pair=t + 1)
                if s % 2:
                    with_ada(u)
                    if u.ada and u.ada[-1][1] == KT - 1:
                        waiting_red.append((u.i, u.ada[-1][0]))
                    nxt[e] = u
            tr = add("trans", na=True, st=1, col=(s % 2) * P, nk=NT, qt=s % 4)
            tr.after = [sc]
            if s % 2:
                pv = add("pv", na=True, pair=t, tile=t, half=s // 4, q0=(s % 4 // 2) * 256, nk=NT,
                         has_turn=True)
                pv.after = [tr, vt]
                ada_red()
        made = nxt or made
    for m in range(KT):
        full("O", "xupd", TX, m, after=[steps[-1]] if m == 0 else (), sect=SECT0[1] + 2, nxT=TX)

    tiles = norm(TX, 2, SECT0[2], 2)
    y = None
    for m in range(KT):
        for j, e in enumerate(["cg", "cv", "cb", "cgate"]):
            y = full("H", e, TX, m, after=tiles if m + j == 0 else ())
    for m in range(KT):
        full("O", "xupd", TX, m, after=[y] if m == 0 else (), sect=SECT0[2] + 2, nxT=TX)

    pool_layer(3, TX, TX)
    add("nstat", T=TX, g=None, sect=None, has_turn=True)
    for k in range(KT):
        add("final", k=k, T=TX)
    for k in range(KT):
        add("sq0", k=k, T=TC, x0=TX)

    for L in range(2):
        both = L == 0
        T = TT if both else TX
        sect = SECT0[4 + L]
        tiles = norm(TT, 4 + L, sect, 4 + L)
        for j in range(5):
            e = "sk" if j == 0 else "sq"
            Tq = TT if j == 0 else T
            u = full("H", e, Tq, j - 1, after=tiles if j == 0 else (), layer=L)
            hn = add("hnorm", T=Tq, what=e, m=j - 1, layer=L, has_turn=True)
            hn.after = [u]
            rp = add("rope", T=Tq, what=e, m=j - 1, layer=L, has_turn=True)
            rp.after = [u]
            qk = rp
        v = full("H", "v", TT, 0, pair=0)
        vt = add("vtrans")
        vt.after = [v]
        for m in range(2):
            full("H", "sf", T, m)
        for m in range(2):
            full("H", "su", T, m)
        for m in range(2):
            u = full("H", "sgv", T, m)
            hn = add("hnorm", T=T, what="sgv", m=m, layer=L, has_turn=True)
            hn.after = [u]
        nts = T // P
        last_in = u
        for m in range(2):
            gt = add("gtrans", T=T, m=m, has_turn=True)
            gt.after = [hn]
            for n0 in range(0, nts, 4):
                sp = add("spgate", T=T, m=m, n0=n0, nn=min(4, nts - n0), layer=L, has_turn=True)
                sp.after = [gt]
            add("gsplit", T=T, m=m)
        ab = []
        for m in range(2):
            for n0 in range(0, nts, 4):
                s = add("four1", m=m, n0=n0, nn=min(4, nts - n0), has_turn=True, in_end=last_in)
                ab.append(s)
        for m in range(2):
            s = add("four2", m=m, T=T, has_turn=True)
            s.after = ab[-1:]
        todo = []
        for m in range(4):
            for half in range(2):
                for qt in range(4):
                    todo.append((m, half, qt, NT))
                if both:
                    for qt in range(4, 6):
                        todo.append((m, half, qt, 2))
        prev = None
        for n in range(len(todo) + 1):
            if n < len(todo):
                m, half, qt, nk = todo[n]
                sc = add("scores", na=False, pair=m, half=half, qt=qt, st=n % 2, eb=n % 2, nk=nk)
                sc.after = [qk]
            if prev is not None:
                (pm, ph, pq, pn), psc = prev
                tr = add("trans", na=False, st=None, eb=(n - 1) % 2, col=(pq % 2) * P, nk=pn, has_turn=True, qt=pq)
                tr.after = [psc]
                if pq % 2:
                    pv = add("pv", na=False, pair=pm, tile=pm, half=ph, q0=(pq - 1) * P, nk=pn, has_turn=True)
                    pv.after = [tr, vt]
            prev = (todo[n], sc) if n < len(todo) else None
        for m in range(KT):
            full("H", "xupd", T, m, after=[steps[-1]] if m == 0 else (), sect=sect + 2, nxT=T)
        tiles = norm(T, 6 + L, sect + 3, 4 + L)
        for c in range(4):
            for m in range(KT):
                h = full("H", "mlp", T, m, after=tiles if c + m == 0 else ())
            for m in range(KT):
                full("M", "xupd", T, m, after=[h] if m == 0 else (), sect=sect + 5,
                     nxT=T if c == 3 and L == 0 else 0)
    turn, w = 0, 0
    for s in steps:
        if s.kind == "upart":
            s.turn, s.w = turn, w
        elif s.kind == "unit":
            if s.ev == "poolmix":
                s.w = w
                if s.grp == 3:
                    w += 1
            else:
                s.w = w
                w += 1
            s.turn = turn
            turn += 1
        elif s.has_turn:
            s.turn = turn
            turn += 1
    a = d = 0
    for s in steps:
        s.a0, s.d0 = a, d
        a += ends_in(s) == "act"
        d += ends_in(s) == "dve"
        s.a1, s.d1 = a, d
    return steps, w




def build_blocks(nc, A, out):
    steps, n_units = plan()
    with ExitStack() as ctx:
        at = [16512]

        def sb(name, shape, dt=F32, offset=None):
            size = int(np.prod(shape[1:])) * 4
            if offset is None:
                offset = at[0]
                at[0] += (size + 31) // 32 * 32
            return nc.alloc_sbuf_tensor_at(name, list(shape), dt, offset=offset)

        Xx = sb("x_lat", [P, KT, TX])
        xc_at = at[0]
        Xc = sb("x_ctx", [P, KT, TC])
        h_at = at[0]
        Hh, Hl = sb("h_hi", [P, KT, TT], F32R), sb("h_lo", [P, KT, TT], F32R)
        RAW = sb("w_raw", [P, 2, D])
        Wh, Wl = sb("w_hi", [P, 2, D], F32R), sb("w_lo", [P, 2, D], F32R)
        ADR = sb("ada_raw", [P, 2, D])
        ACC = sb("ada_acc", [P, 2, D])
        T = []
        for n in range(4):
            T.append(sb(f"tmp{n + 1}", [P, UW]))
        T1, T2, T3, T4 = T
        IDN, ONES, BONES, PERM = (sb(n, [P, P]) for n in ("ident", "ones", "head_ones", "rope_swap"))
        CS = sb("dft64", [P, 2 * P])
        MOD = sb("modulation", [P, N_SECT, 2, KT])
        ADAB = sb("ada_bias", [P, N_SECT, KT])
        NG = sb("norm_gains", [P, 9, KT])
        CV, CVT, SC = sb("cond", [P, 4, KT]), sb("cond_tanh", [P, 4, KT]), sb("cond_silu", [P, 4, KT])
        PSC = sb("pool_scale", [P, 2, KT])
        CW = sb("conv_cols", [P, 4, KT])
        HG = sb("head_gains", [P, 2, 4])
        EDGE = sb("pool_edges", [P, 4, 2, PADL])
        GA = sb("gain_cols", [P, 2, KT])
        ST = sb("softmax_stats", [P, 2, 8])
        EPSC = sb("eps", [P, 1])
        ar = at[0]

        def arena(name, shape, dt, off):
            return sb(name, shape, dt, ar + off)

        K1 = 1024
        HOT, STAGE, RPB = arena("onehot", [32, 4096], F32, 0), arena("bias_out", [P, 2, 512], F32, 16384), arena("rpb", [32, 240], F32, 20480)
        Dh, Dl = arena("d_hi", [P, KT, TT], F32R, 0), arena("d_lo", [P, KT, TT], F32R, 24 * K1)
        G, U = arena("gate", [P, KT, TT], F32, 48 * K1), arena("u_padded", [P, UW], F32, 72 * K1)
        Oh, Ol = arena("o_hi", [P, KT, TX], F32R, 0), arena("o_lo", [P, KT, TX], F32R, 16 * K1)
        PTh, PTl = arena("pt_hi", [P, NT, 256], F32R, 32 * K1), arena("pt_lo", [P, NT, 256], F32R, 38 * K1)
        Qh, Ql = arena("q_hi", [P, 2, TX], F32R, 44 * K1), arena("q_lo", [P, 2, TX], F32R, 48 * K1)
        Kh, Kl = arena("k_hi", [P, 2, TT], F32R, 52 * K1), arena("k_lo", [P, 2, TT], F32R, 58 * K1)
        Vh, Vl = arena("v_hi", [P, NT, P], F32R, 64 * K1), arena("v_lo", [P, NT, P], F32R, 67 * K1)
        G2 = arena("na_gate", [P, 2, TX], F32, 70 * K1)
        BIAS = [sb(f"bias{n}", [P, 14 * GRID_W], F32, xc_at + n * 3584) for n in range(2)]
        Z = arena("conv_in", [P, TX + 2], F32, 70 * K1)
        SQh, SQl = arena("sq_hi", [P, 4, TT], F32R, 0), arena("sq_lo", [P, 4, TT], F32R, 12 * K1)
        SKh, SKl = arena("sk_hi", [P, TT], F32R, 24 * K1), arena("sk_lo", [P, TT], F32R, 27 * K1)
        F = arena("fourier_in", [P, 2, TT], F32, 44 * K1)
        SU = arena("gmlp_u", [P, 2, TT], F32, 50 * K1)
        GV = arena("gmlp_v", [P, 2, TT], F32, 56 * K1)
        GT = arena("gmlp_vt", [P, NT, P], F32, 32 * K1)
        AB = arena("fourier_mid", [P, NT, 2, 256], F32, 32 * K1)
        EX1 = arena("exp1", [P, TT], F32, 44 * K1)
        VSh, VSl = Vh, Vl
        ROPC, ROPS = arena("rope_cos", [P, TX], F32, 70 * K1), arena("rope_sin", [P, TX], F32, 72 * K1)
        WS, BS = arena("w_spatial", [P, 512], F32, 74 * K1), arena("b_spatial", [P, 2, P], F32, 30 * K1)
        DC = sb("dft_cos", [P, 4, TX], F32, h_at)
        DS = sb("dft_sin", [P, 4, TX], F32, h_at + KT * TT * 4)
        Mh, Ml = arena("m_hi", [P, KT, TT], F32R, 0), arena("m_lo", [P, KT, TT], F32R, 24 * K1)
        EX = [T4, EX1]
        bias_d = nc.dram_tensor("bias_table", [240, GRID_W, GRID_W], F32, kind="Internal").ap()

        PS = ctx.enter_context(nc.psum_tensor("turns", [P, 2, 1024], F32))
        SP_ = ctx.enter_context(nc.psum_tensor("scores", [P, 2, 1024], F32))

        def sem(name):
            return ctx.enter_context(nc.semaphore(name))

        raw_landed = [sem(f"raw_landed{n}") for n in range(2)]
        w_rounded, w_split = sem("w_rounded"), sem("w_split")
        ada_landed = [sem(f"ada_landed{n}") for n in range(2)]
        ada_done = sem("ada_done")
        turn_mm = sem("turn_mm")
        score_mm = [sem(f"score_mm{n}") for n in range(2)]
        act_done, dve_done = sem("act_done"), sem("dve_done")
        for_dve, for_act = sem("piece_for_dve"), sem("piece_for_act")
        act_own, dve_own = sem("act_own"), sem("dve_own")
        consts_in, x_in, hot_in = sem("consts_in"), sem("x_in"), sem("hot_in")
        bias_out = [sem(f"bias_out{n}") for n in range(2)]
        bias_in = [sem(f"bias_in{n}") for n in range(2)]
        ctx2_in, dft_in, sp_in, out_done = sem("ctx2_in"), sem("dft_in"), sem("sp_in"), sem("out_done")

        turn_of_w = {}
        for s in steps:
            if s.kind == "unit":
                turn_of_w[s.w] = s.turn
        red_turn = {s.sect: s.turn for s in steps if s.kind == "adared"}
        step_of_turn = {s.turn: s for s in steps if s.turn is not None and s.kind != "upart"}
        by_kind = {}
        for s in steps:
            by_kind.setdefault(s.kind, []).append(s)
        na_scores = [s for s in by_kind["scores"] if s.na]
        s_scores_end = na_scores[-1]
        heads_na = [na_scores[i * 4:i * 4 + 4] for i in range(NHEADS_NA)]
        first_ctx2 = [s for s in by_kind["sq0"] if s.x0 == TX][0]
        na_norm_end = [s for s in by_kind["ntile"] if s.g == 1][-1]
        four_first = [s for s in by_kind["four1"] if s.m == 0 and s.n0 == 0]
        sk_steps = [s for s in by_kind["unit"] if s.ev == "sk"]

        def segs(t):
            return [(0, TX)] if t == TX else [(0, TX), (TX, TC)]

        def xseg(lo, m):
            return Xx[:, m, :] if lo == 0 else Xc[:, m, :]

        block = ctx.enter_context(nc.Block())

        @block.sync
        def _(sp):
            for dst, src in ((IDN, "ident"), (ONES, "ones"), (BONES, "bones"), (PERM, "perm"), (CS, "dft64"), (ADAB, "adab"),
                             (NG, "normg"), (CV, "cond"), (PSC, "psc"), (CW, "cw"), (HG, "hg"), (EDGE, "edge")):
                sp.dma_start(dst[:], A[src]).then_inc(consts_in, 16)
            sp.dma_start(HOT[:], A["onehot"]).then_inc(hot_in, 16)
            sp.dma_start(RPB[:], A["rpb"]).then_inc(hot_in, 16)
            sp.dma_start(Xx[:], A["xT"].rearrange("(k p) t -> p k t", p=P)).then_inc(x_in, 16)
            sp.dma_start(Xc[:], A["ctxT"].rearrange("(k p) t -> p k t", p=P)).then_inc(x_in, 16)
            chunk = 0
            sent = 0
            for s in steps:
                if s.kind in ("unit", "upart") and s.w == sent:
                    if sent >= 2:
                        sp.wait_ge(w_split, sent - 1)
                    sp.dma_start(RAW[:, sent % 2, :], A["wpack"][sent]).then_inc(raw_landed[sent % 2], 16)
                    sent += 1
                for _ in s.ada:
                    if chunk >= 2:
                        sp.wait_ge(ada_done, chunk - 1)
                    sp.dma_start(ADR[:, chunk % 2, :], A["adapack"][chunk]).then_inc(ada_landed[chunk % 2], 16)
                    chunk += 1
                if s is na_norm_end or (s.kind == "scores" and s.na and s.first):
                    if s is na_norm_end:
                        sp.wait_ge(dve_done, s.d1)
                        for n in range(2):
                            sp.wait_ge(bias_out[n], 16 * 8)
                        heads = [0]
                    else:
                        n = s.pair * 2 + s.half + 1
                        heads = [n] if n < NHEADS_NA else []
                        if n >= 2 and heads:
                            sp.wait_ge(dve_done, heads_na[n - 2][-1].d1)
                    for n in heads:
                        for r in range(2):
                            sp.dma_start(BIAS[n % 2][r * 64:r * 64 + 64, :].rearrange("c (s j) -> c s j", j=GRID_W),
                                         bias_d[n * NDR + 1 - r:n * NDR + 15 - r].rearrange("s c j -> c s j")
                                         ).then_inc(bias_in[n % 2], 16)
                if s is first_ctx2:
                    sp.wait_ge(dve_done, s_scores_end.d1)
                    sp.dma_start(Xc[:], A["ctxT_2"].rearrange("(k p) t -> p k t", p=P)).then_inc(ctx2_in, 16)
                if s in sk_steps:
                    L = sk_steps.index(s)
                    sp.wait_ge(dve_done, s.after[0].d1)
                    sp.dma_start(ROPC[:], A["rope_cos"]).then_inc(sp_in, 16)
                    sp.dma_start(ROPS[:], A["rope_sin"]).then_inc(sp_in, 16)
                    sp.dma_start(WS[:], A["wsp"][L]).then_inc(sp_in, 16)
                    sp.dma_start(BS[:], A["bsp"][L]).then_inc(sp_in, 16)
                if s in four_first:
                    sp.wait_ge(turn_mm, s.in_end.turn + 1)
                    sp.dma_start(DC[:], A["dft_cos"]).then_inc(dft_in, 16)
                    sp.dma_start(DS[:], A["dft_sin"]).then_inc(dft_in, 16)
            sp.wait_ge(dve_done, steps[-1].d1)
            sp.dma_start(out.rearrange("(k p) t -> p k t", p=P), Xx[:]).then_inc(out_done, 16)
            sp.wait_ge(out_done, 16)

        @block.gpsimd
        def _(pool):
            for w in range(n_units):
                b = w % 2
                pool.wait_ge(raw_landed[b], 16 * (w // 2 + 1))
                if w >= 2:
                    pool.wait_ge(turn_mm, turn_of_w[w - 2] + 1)
                pool.tensor_scalar(Wh[:, b, :], RAW[:, b, :], 1.0, None, ALU.mult).then_inc(w_rounded, 1)
                pool.wait_ge(w_rounded, w + 1)
                pool.tensor_tensor(Wl[:, b, :], RAW[:, b, :], Wh[:, b, :].bitcast(F32), ALU.subtract).then_inc(w_split, 1)

        @block.tensor
        def _(pe):
            def wait_steps(after):
                a = max([x.a1 for x in after if ends_in(x) == "act"], default=0)
                d = max([x.d1 for x in after if ends_in(x) == "dve"], default=0)
                if a:
                    pe.wait_ge(act_done, a)
                if d:
                    pe.wait_ge(dve_done, d)

            def free_turn(s):
                if s.turn >= 2:
                    wait_steps([step_of_turn[s.turn - 2]])

            last_scores = [None, None]

            def free_scores(b, s):
                if last_scores[b] is not None:
                    wait_steps([last_scores[b]])
                last_scores[b] = s

            src_of = {"H": (Hh, Hl), "O": (Oh, Ol), "M": (Mh, Ml), "D": (Dh, Dl)}

            def three_pass(dst, wh, wl, xh, xl, t, first, last):
                for n, (w, x) in enumerate(((wh, xh), (wh, xl), (wl, xh))):
                    for lo, sz in segs(t):
                        ins = pe.matmul(dst[:, lo:lo + sz], w, x[:, lo:lo + sz], start=first and n == 0,
                                        stop=last and n == 2)
                return ins

            def unit(s):
                b = s.turn % 2
                if s.part != 1:
                    pe.wait_ge(w_split, s.w + 1)
                    free_turn(s)
                xh, xl = src_of[s.src]
                ks = range(KT) if s.part is None else range(s.part * 4, s.part * 4 + 4)
                if s.ev == "poolmix":
                    ks = range(2)
                if s.after and len(s.after) < KT:
                    wait_steps(s.after)
                for k in ks:
                    if len(s.after) == KT:
                        wait_steps(s.after[k:k + 1])
                    col = (s.grp * 2 + k if s.ev == "poolmix" else k) * P
                    tile = s.m // 2 * 2 + k if s.ev == "poolmix" else k
                    ins = three_pass(PS[:, b, :], Wh[:, s.w % 2, col:col + P], Wl[:, s.w % 2, col:col + P],
                                     xh[:, tile, :], xl[:, tile, :], s.T, k == 0, k == (1 if s.ev == "poolmix" else KT - 1))
                if s.part != 0:
                    ins.then_inc(turn_mm, 1)

            for s in steps:
                b = None if s.turn is None else s.turn % 2
                if s.kind in ("unit", "upart"):
                    unit(s)
                elif s.kind == "bias_row":
                    if s.g == 0 and s.c == 0:
                        pe.wait_ge(hot_in, 32)
                    free_turn(s)
                    pe.matmul(PS[0:120, b, 0:512], RPB[:, s.g * 120:s.g * 120 + 120], HOT[:, s.c * 512:s.c * 512 + 512],
                              start=True, stop=True).then_inc(turn_mm, 1)
                elif s.kind == "adared":
                    if s.sect == 0:
                        pe.wait_ge(consts_in, 16 * 12)
                    pe.wait_ge(ada_done, KT * (s.sect + 1))
                    free_turn(s)
                    for c in range(1 + (s.sect in CTX_SECT)):
                        for j in range(KT):
                            ins = pe.matmul(PS[:, b, c * KT + j:c * KT + j + 1], ACC[:, c, j * P:j * P + P], ONES[:, 0:1],
                                            start=True, stop=True)
                    ins.then_inc(turn_mm, 1)
                elif s.kind == "nstat":
                    pe.wait_ge(dve_done, s.d0)
                    free_turn(s)
                    for lo, sz in segs(s.T):
                        ins = pe.matmul(PS[:, b, lo:lo + sz], ONES[:], T4[:, lo:lo + sz], start=True, stop=True)
                    ins.then_inc(turn_mm, 1)
                elif s.kind == "hnorm":
                    wait_steps(s.after)
                    free_turn(s)
                    for lo, sz in segs(s.T):
                        ins = pe.matmul(PS[:, b, lo:lo + sz], BONES[:], T2[:, lo:lo + sz], start=True, stop=True)
                    ins.then_inc(turn_mm, 1)
                elif s.kind == "rope":
                    free_turn(s)
                    pe.matmul(PS[:, b, 0:TX], PERM[:], T1[:, 0:TX], start=True, stop=True).then_inc(turn_mm, 1)
                elif s.kind == "vtrans":
                    wait_steps(s.after)
                    free_scores(1, s)
                    for n in range(NT):
                        ins = pe.transpose(SP_[:, 1, n * P:n * P + P], T3[:, n * P:n * P + P], IDN[:])
                    ins.then_inc(score_mm[1], 1)
                elif s.kind == "scores":
                    wait_steps(s.after)
                    free_scores(s.st, s)
                    r = slice(64 * s.half, 64 * s.half + 64)
                    q = slice(s.qt * P, s.qt * P + P)
                    if s.na:
                        qh, ql, kh, kl = (x[r, s.pair % 2] for x in (Qh, Ql, Kh, Kl))
                    else:
                        qh, ql, kh, kl = SQh[r, s.pair], SQl[r, s.pair], SKh[r], SKl[r]
                    for n, (x, y) in enumerate(((qh, kh), (qh, kl), (ql, kh))):
                        if s.nk == NT:
                            for lo, sz in segs(TT):
                                ins = pe.matmul(SP_[:, s.st, lo:lo + sz], x[:, q], y[:, lo:lo + sz], start=n == 0, stop=n == 2)
                        else:
                            ins = pe.matmul(SP_[:, s.st, 0:TC], x[:, q], y[:, TX:TT], start=n == 0, stop=n == 2)
                    ins.then_inc(score_mm[s.st], 1)
                elif s.kind == "trans":
                    wait_steps(s.after)
                    if s.na:
                        free_scores(1, s)
                        dst, src = SP_[:, 1, :], T4
                    else:
                        free_turn(s)
                        dst, src = PS[:, b, :], EX[s.eb]
                    for n in range(s.nk):
                        ins = pe.transpose(dst[:, n * P:n * P + P], src[:, n * P:n * P + P], IDN[:])
                    ins.then_inc(score_mm[1] if s.na else turn_mm, 1)
                elif s.kind == "pv":
                    wait_steps(s.after)
                    free_turn(s)
                    k0 = NT - s.nk
                    for n in range(s.nk):
                        for j, (v, p) in enumerate(((Vh, PTh), (Vh, PTl), (Vl, PTh))):
                            ins = pe.matmul(PS[:, b, 0:256], v[:, k0 + n, :], p[:, n, :], start=n + j == 0,
                                            stop=n == s.nk - 1 and j == 2)
                    ins.then_inc(turn_mm, 1)
                elif s.kind == "gtrans":
                    wait_steps(s.after)
                    free_turn(s)
                    for n in range(s.T // P):
                        ins = pe.transpose(PS[:, b, n * P:n * P + P], GV[:, s.m, n * P:n * P + P], IDN[:])
                    ins.then_inc(turn_mm, 1)
                elif s.kind == "spgate":
                    wait_steps(s.after)
                    free_turn(s)
                    pe.wait_ge(sp_in, 64 * (s.layer + 1))
                    for n in range(s.nn):
                        ins = pe.matmul(PS[:, b, n * 256:n * 256 + 256], GT[:, s.n0 + n, :], WS[:, s.m * 256:s.m * 256 + 256],
                                        start=True, stop=True)
                    ins.then_inc(turn_mm, 1)
                elif s.kind == "four1":
                    pe.wait_ge(act_done, s.a0)
                    free_turn(s)
                    for n in range(s.nn):
                        c = (s.n0 + n) * P
                        ins = pe.matmul(PS[:, b, n * 256:n * 256 + 256], F[:, s.m, c:c + P], CS[:], start=True, stop=True)
                    ins.then_inc(turn_mm, 1)
                elif s.kind == "four2":
                    wait_steps(s.after)
                    free_turn(s)
                    done_l = sum(x.i < s.i for x in four_first)
                    pe.wait_ge(dft_in, 32 * done_l)
                    for n in range(4):
                        for j, tab in enumerate((DC, DS)):
                            ins = pe.matmul(PS[:, b, 0:TX], AB[:, n, s.m, j * P:j * P + P], tab[:, n, :], start=n + j == 0,
                                            stop=n + j == 4)
                    if s.T == TT:
                        for n in range(2):
                            for j, tab in enumerate((DC, DS)):
                                ins = pe.matmul(PS[:, b, TX:TT], AB[:, 4 + n, s.m, j * P:j * P + P], tab[:, n, 0:TX:2],
                                                start=n + j == 0, stop=n + j == 2)
                    ins.then_inc(turn_mm, 1)

        @block.scalar
        def _(act):
            given, taken, own = [0], [0], [0]
            filled = [0, 0]

            def give(ins):
                given[0] += 1
                ins.then_inc(for_dve, 1)

            def take():
                taken[0] += 1
                act.wait_ge(for_act, taken[0])

            def chain(ins):
                own[0] += 1
                ins.then_inc(act_own, 1)
                act.wait_ge(act_own, own[0])

            def done(ins):
                ins.then_inc(act_done, 1)

            def scores_in(b):
                filled[b] += 1
                act.wait_ge(score_mm[b], filled[b])

            for s in steps:
                if s.kind in ("upart", "adastep", "adared", "pool", "spgate"):
                    continue
                if s.kind == "unit" and (s.ev in DVE_ONLY or (s.ev == "xupd" and not s.nxT)):
                    if s.ev == "cv" or s.ev == "cb" or s.ev == "xupd":
                        continue
                if s.d0:
                    act.wait_ge(dve_done, s.d0)
                if s.a0:
                    act.wait_ge(act_done, s.a0)
                b = None if s.turn is None else s.turn % 2
                ps = None if b is None else PS[:, b, :]
                t = s.T
                if s.turn is not None and not (s.kind == "unit" and s.ev == "xupd"):
                    act.wait_ge(turn_mm, s.turn + 1)
                if s.kind == "silu_c":
                    act.wait_ge(consts_in, 16 * 12)
                    give(act.activation(CVT[:], CV[:], ACT.Tanh, scale=0.5))
                elif s.kind == "bias_row":
                    n = s.g * 8 + s.c
                    if n >= 2:
                        act.wait_ge(bias_out[n % 2], 16 * (n // 2))
                    done(act.activation(STAGE[0:120, n % 2, :], PS[0:120, b, 0:512], ACT.Copy))
                    act.wait_ge(act_done, s.a1)
                    act.dma_start(bias_d[s.g * 120:s.g * 120 + 120, s.c * 8:s.c * 8 + 8, :].rearrange("h c j -> h (c j)"),
                                  STAGE[0:120, n % 2, :]).then_inc(bias_out[n % 2], 16)
                elif s.kind == "sq0":
                    if s.k == 0 and s.x0 == 0:
                        act.wait_ge(x_in, 32)
                        for n in range(2):
                            act.wait_ge(bias_out[n], 16 * 8)
                    if s.k == 0 and s.x0 == TX:
                        act.wait_ge(ctx2_in, 16)
                    for lo, sz in ([(TX, TC)] if s.x0 else segs(TT)):
                        ins = act.activation(T1[:, lo:lo + sz], xseg(lo, s.k), ACT.Square)
                    give(ins)
                elif s.kind == "nstat":
                    give(act.activation(T3[:, 0:t], ps[:, 0:t], ACT.Sqrt, bias=EPSC[:], scale=1.0 / D))
                elif s.kind == "ntile":
                    take()
                    src = (T1, T2)[s.k % 2]
                    for c, (lo, sz) in enumerate(segs(t)):
                        ins = act.activation(Hh[:, s.k, lo:lo + sz], src[:, lo:lo + sz], ACT.Identity,
                                             bias=MOD[:, s.sect, c, s.k:s.k + 1], scale=1.0)
                    give(ins)
                elif s.kind == "final":
                    take()
                    give(act.activation(T1[:, 0:t], Xx[:, s.k, :], ACT.Square))
                elif s.kind == "hnorm":
                    give(act.activation(T3[:, 0:t], ps[:, 0:t], ACT.Sqrt, bias=EPSC[:], scale=1.0 / 64))
                elif s.kind == "rope":
                    take()
                    if s.what == "sk":
                        dst = SKh[:, 0:t]
                    else:
                        dst = SQh[:, s.m, 0:t]
                    give(act.activation(dst, T2[:, 0:t], ACT.Copy))
                elif s.kind == "vtrans":
                    scores_in(1)
                    give(act.activation(Vh[:], SP_[:, 1, 0:TT].rearrange("p (n f) -> p n f", f=P), ACT.Copy))
                elif s.kind == "scores":
                    ex = T4 if s.na else EX[s.eb]
                    st = ST[:, s.qt % 2, :]
                    take()
                    if s.na:
                        act.activation(ex[:, 0:TX], ex[:, 0:TX], ACT.Exp, bias=st[:, 2:3], scale=1.0, accum_out=st[:, 3:4])
                        scores_in(0)
                        give(act.activation(ex[:, TX:TT], SP_[:, 0, TX:TT], ACT.Exp, bias=st[:, 2:3], scale=1.0,
                                            accum_out=st[:, 4:5]))
                    else:
                        nk = s.nk * P
                        scores_in(s.st)
                        give(act.activation(ex[:, 0:nk], SP_[:, s.st, 0:nk], ACT.Exp, bias=st[:, 2:3], scale=1.0,
                                            accum_out=st[:, 3:4]))
                elif s.kind == "trans":
                    if s.na:
                        scores_in(1)
                        src = SP_[:, 1, 0:TT]
                    else:
                        src = ps[:, 0:s.nk * P]
                    give(act.activation(PTh[:, 0:s.nk, s.col:s.col + P], src.rearrange("p (n q) -> p n q", q=P), ACT.Copy))
                elif s.kind == "pv":
                    r = slice(64 * s.half, 64 * s.half + 64)
                    if s.na:
                        take()
                        give(act.activation(Oh[r, s.tile, s.q0:s.q0 + 256], T2[r, 0:256], ACT.Copy))
                    else:
                        give(act.activation(Hh[r, s.tile, s.q0:s.q0 + 256], ps[r, 0:256], ACT.Copy))
                elif s.kind == "gtrans":
                    done(act.activation(GT[:, 0:t // P, :], ps[:, 0:t].rearrange("p (n f) -> p n f", f=P), ACT.Copy))
                elif s.kind == "gsplit":
                    take()
                    give(act.activation(Hh[:, 6 + s.m, 0:t], T2[:, 0:t], ACT.Copy))
                elif s.kind == "four1":
                    done(act.activation(AB[:, s.n0:s.n0 + s.nn, s.m, :],
                                        ps[:, 0:s.nn * 256].rearrange("p (n f) -> p n f", f=256), ACT.Copy))
                elif s.kind == "four2":
                    for lo, sz in segs(t):
                        ins = act.activation(Hh[:, 4 + s.m, lo:lo + sz], ps[:, lo:lo + sz], ACT.Copy, scale=four_scale(sz))
                    give(ins)
                else:
                    assert s.kind == "unit", s.kind
                    m = s.m
                    if s.ev == "u":
                        for lo, sz in segs(t):
                            o = PADL if lo == 0 else UC + PADL
                            ins = act.activation(U[:, o:o + sz], ps[:, lo:lo + sz], ACT.Copy)
                        done(ins)
                    elif s.ev in ("gate", "g", "cgate"):
                        give(act.activation(T1[:, 0:t], ps[:, 0:t], ACT.Tanh, scale=0.5))
                        if s.ev == "cgate":
                            take()
                            give(act.activation(Oh[:, m, :], T2[:, 0:t], ACT.Copy))
                    elif s.ev == "poolmix":
                        take()
                        give(act.activation(Hh[:, m, 0:t], T2[:, 0:t], ACT.Copy))
                    elif s.ev == "xupd":
                        take()
                        for lo, sz in segs(s.nxT):
                            ins = act.activation(T1[:, lo:lo + sz], xseg(lo, m), ACT.Square)
                        give(ins)
                    elif s.ev in ("q", "k"):
                        dst = (Qh if s.ev == "q" else Kh)[:, s.pair % 2, 0:t]
                        give(act.activation(dst, ps[:, 0:t], ACT.Copy, scale=0.125 if s.ev == "q" else 1.0))
                    elif s.ev in ("v", "cg"):
                        done(act.activation(T3[:, 0:t], ps[:, 0:t], ACT.Copy))
                    elif s.ev in ("sk", "sq"):
                        g = HG[:, s.layer, 1:2] if s.ev == "sk" else HG[:, s.layer, 0:1]
                        act.activation(T1[:, 0:t], ps[:, 0:t], ACT.Copy, scale=g)
                        done(act.activation(T2[:, 0:t], ps[:, 0:t], ACT.Square))
                    elif s.ev == "sf":
                        done(act.activation(F[:, m, 0:t], ps[:, 0:t], ACT.Copy))
                    elif s.ev in ("su", "sgv"):
                        give(act.activation(T1[:, 0:t], ps[:, 0:t], ACT.Square))
                        take()
                        give(act.activation(T1[:, 0:t], T2[:, 0:t], ACT.Tanh, scale=GELU_C))
                    elif s.ev == "mlp":
                        chain(act.activation(T1[:, 0:t], ps[:, 0:t], ACT.Relu))
                        give(act.activation(Mh[:, m, 0:t], T1[:, 0:t], ACT.Square))

        @block.vector
        def _(dve):
            taken, own = [0], [0]
            filled = [0, 0]
            chunk = [0]

            def give(ins):
                ins.then_inc(for_act, 1)

            def take():
                taken[0] += 1
                dve.wait_ge(for_dve, taken[0])

            def chain(ins):
                own[0] += 1
                ins.then_inc(dve_own, 1)
                dve.wait_ge(dve_own, own[0])

            def done(ins):
                ins.then_inc(dve_done, 1)

            def scores_in(b):
                filled[b] += 1
                dve.wait_ge(score_mm[b], filled[b])

            def tt(dst, x, y, op):
                return dve.tensor_tensor(dst, x, y, op)

            def stt(dst, x, c, y, op0, op1):
                return dve.scalar_tensor_tensor(out=dst, in0=x, scalar=c, in1=y, op0=op0, op1=op1)

            def ada_chunk(sect, k):
                n = chunk[0]
                dve.wait_ge(ada_landed[n % 2], 16 * (n // 2 + 1))
                if n:
                    dve.wait_ge(ada_done, n)
                if k == 0 and sect:
                    dve.wait_ge(turn_mm, red_turn[sect - 1] + 1)
                base = 0 if sect < 12 else 2
                for c in range(1 + (sect in CTX_SECT)):
                    w = SC[:, base + c, k:k + 1]
                    if k == 0:
                        ins = dve.tensor_scalar(ACC[:, c, :], ADR[:, n % 2, :], w, None, ALU.mult)
                    else:
                        ins = stt(ACC[:, c, :], ADR[:, n % 2, :], w, ACC[:, c, :], ALU.mult, ALU.add)
                ins.then_inc(ada_done, 1)
                chunk[0] += 1

            def normed(s, k):
                dst = (T1, T2)[k % 2]
                for c, (lo, sz) in enumerate(segs(s.T)):
                    ins = stt(dst[:, lo:lo + sz], xseg(lo, k), GA[:, c, k:k + 1], T3[:, lo:lo + sz], ALU.mult, ALU.mult)
                give(ins)

            def sum_squares(k, parts):
                for lo, sz in parts:
                    if k == 0:
                        ins = dve.tensor_copy(T4[:, lo:lo + sz], T1[:, lo:lo + sz])
                    else:
                        ins = tt(T4[:, lo:lo + sz], T4[:, lo:lo + sz], T1[:, lo:lo + sz], ALU.add)
                return ins

            def window_means(s):
                w = WINDOWS[s.m // 2]
                chain(tt(T1[:, 1:UW], U[:, 0:UW - 1], U[:, 1:UW], ALU.add))
                cur, lo, hi, width = T1, 1, UW, 2
                while width < w:
                    d = width // 2
                    nxt = T2 if cur is T1 else T1
                    lo, hi = lo + d, hi - d
                    chain(tt(nxt[:, lo:hi], cur[:, lo - d:hi - d], cur[:, lo + d:hi + d], ALU.add))
                    cur, width = nxt, width * 2
                parts = [(PADL, 0, TX)] + ([(UC + PADL, TX, TC)] if s.T == TT else [])
                for o, _, sz in parts:
                    for j, q in enumerate((o, o + sz - PADL)):
                        ins = tt(cur[:, q:q + PADL], cur[:, q:q + PADL], EDGE[:, s.m // 2, j, :], ALU.mult)
                chain(ins)
                f = T2 if cur is T1 else T1
                for o, lo, sz in parts:
                    ins = stt(f[:, lo:lo + sz], cur[:, o:o + sz], 1.0 / w, U[:, o:o + sz], ALU.mult, ALU.subtract)
                chain(ins)
                chain(dve.tensor_copy(Dh[:, s.m, 0:s.T], f[:, 0:s.T]))
                done(tt(Dl[:, s.m, 0:s.T], f[:, 0:s.T], Dh[:, s.m, 0:s.T].bitcast(F32), ALU.subtract))

            def rest(lo_dst, src, hi, scale=None):
                if scale is None:
                    return tt(lo_dst, src, hi.bitcast(F32), ALU.subtract)
                return stt(lo_dst, src, scale, hi.bitcast(F32), ALU.mult, ALU.subtract)

            chain(dve.memset(EPSC[:], EPS))
            chain(dve.memset(U[:], 0.0))
            for s in steps:
                b = None if s.turn is None else s.turn % 2
                ps = None if b is None else PS[:, b, :]
                t = s.T
                if ends_in(s) == "dve":
                    if s.a0:
                        dve.wait_ge(act_done, s.a0)
                    if s.d0:
                        dve.wait_ge(dve_done, s.d0)
                    if s.turn is not None:
                        dve.wait_ge(turn_mm, s.turn + 1)
                if s.kind == "silu_c":
                    dve.wait_ge(consts_in, 16 * 12)
                    dve.tensor_scalar(PSC[:], PSC[:], 0.5, None, ALU.mult)
                    dve.tensor_scalar(HG[:, :, 2:4], HG[:, :, 2:4], 0.5, None, ALU.mult)
                    take()
                    chain(stt(CVT[:], CVT[:], 1.0, CV[:], ALU.add, ALU.mult))
                    done(dve.tensor_scalar(SC[:], CVT[:], 0.5, None, ALU.mult))
                elif s.kind == "adared":
                    n = 1 + (s.sect in CTX_SECT)
                    for c in range(n):
                        ins = tt(MOD[:, s.sect, c, :], ps[:, c * KT:c * KT + KT], ADAB[:, s.sect, :], ALU.add)
                    done(ins)
                elif s.kind == "sq0":
                    take()
                    done(sum_squares(s.k, [(TX, TC)] if s.x0 else segs(TT)))
                elif s.kind == "nstat":
                    take()
                    if s.g is not None:
                        for c in range(1 + (t == TT)):
                            ins = stt(GA[:, c, :], MOD[:, s.sect + 1, c, :], 1.0, NG[:, s.g, :], ALU.add, ALU.mult)
                        if s.g == 3:
                            dve.memset(U[:], 0.0)
                    done(dve.reciprocal(T3[:, 0:t], T3[:, 0:t]))
                elif s.kind == "ntile":
                    if s.k == 0:
                        normed(s, 0)
                    if s.k < KT - 1:
                        normed(s, s.k + 1)
                    take()
                    src = (T1, T2)[s.k % 2]
                    for c, (lo, sz) in enumerate(segs(t)):
                        ins = stt(Hl[:, s.k, lo:lo + sz], src[:, lo:lo + sz], MOD[:, s.sect, c, s.k:s.k + 1],
                                  Hh[:, s.k, lo:lo + sz].bitcast(F32), ALU.add, ALU.subtract)
                    done(ins)
                elif s.kind == "final":
                    give(stt(Xx[:, s.k, :], Xx[:, s.k, :], NG[:, 8, s.k:s.k + 1], T3[:, 0:t], ALU.mult, ALU.mult))
                    take()
                    done(sum_squares(s.k, segs(TX)))
                elif s.kind == "pool":
                    window_means(s)
                elif s.kind == "hnorm":
                    take()
                    if s.what == "sgv":
                        chain(dve.reciprocal(T3[:, 0:t], T3[:, 0:t]))
                        done(stt(GV[:, s.m, 0:t], GV[:, s.m, 0:t], HG[:, s.layer, 2 + s.m:3 + s.m], T3[:, 0:t],
                                 ALU.mult, ALU.mult))
                    else:
                        done(dve.reciprocal(T3[:, 0:t], T3[:, 0:t]))
                elif s.kind == "rope":
                    if s.what == "sk":
                        dve.wait_ge(sp_in, 64 * (s.layer + 1))
                    tt(T4[:, 0:TX], T1[:, 0:TX], ROPC[:], ALU.mult)
                    chain(tt(T2[:, 0:TX], ps[:, 0:TX], ROPS[:], ALU.mult))
                    chain(tt(T4[:, 0:TX], T4[:, 0:TX], T2[:, 0:TX], ALU.add))
                    c = 1.0 if s.what == "sk" else 0.125
                    ins = stt(T2[:, 0:TX], T4[:, 0:TX], c, T3[:, 0:TX], ALU.mult, ALU.mult)
                    if t == TT:
                        ins = stt(T2[:, TX:TT], T1[:, TX:TT], c, T3[:, TX:TT], ALU.mult, ALU.mult)
                    give(ins)
                    take()
                    hi, lo = (SKh[:, 0:t], SKl[:, 0:t]) if s.what == "sk" else (SQh[:, s.m, 0:t], SQl[:, s.m, 0:t])
                    done(rest(lo, T2[:, 0:t], hi))
                elif s.kind == "vtrans":
                    scores_in(1)
                    take()
                    done(rest(Vl[:], SP_[:, 1, 0:TT].rearrange("p (n f) -> p n f", f=P), Vh[:]))
                elif s.kind == "scores":
                    ex = T4 if s.na else EX[s.eb]
                    st = ST[:, s.qt % 2, :]
                    nk = s.nk * P
                    scores_in(s.st)
                    if s.na:
                        if s.first:
                            h = s.pair * 2 + s.half
                            dve.wait_ge(bias_in[h % 2], 32 * (h // 2 + 1))
                        bias = BIAS[(s.pair * 2 + s.half) % 2][:, (6 - 2 * s.qt) * 64:(14 - 2 * s.qt) * 64]
                        dve.tensor_tensor_reduce(ex[:, 0:TX], SP_[:, 0, 0:TX], bias, 1.0, -3.0e38, ALU.add, ALU.max, st[:, 0:1])
                        chain(dve.tensor_reduce(st[:, 1:2], SP_[:, 0, TX:TT], AX.X, ALU.max))
                        give(dve.tensor_scalar(st[:, 2:3], st[:, 0:1], st[:, 1:2], -1.0, ALU.max, ALU.mult))
                        take()
                        chain(tt(st[:, 5:6], st[:, 3:4], st[:, 4:5], ALU.add))
                        chain(dve.reciprocal(st[:, 6:7], st[:, 5:6]))
                    else:
                        give(dve.tensor_reduce(st[:, 2:3], SP_[:, s.st, 0:nk], AX.X, ALU.max, negate=True))
                        take()
                        chain(dve.reciprocal(st[:, 6:7], st[:, 3:4]))
                    done(dve.tensor_scalar(ex[:, 0:nk], ex[:, 0:nk], st[:, 6:7], None, ALU.mult))
                elif s.kind == "trans":
                    if s.na:
                        scores_in(1)
                        src = SP_[:, 1, 0:TT]
                    else:
                        src = ps[:, 0:s.nk * P]
                    take()
                    done(rest(PTl[:, 0:s.nk, s.col:s.col + P], src.rearrange("p (n q) -> p n q", q=P),
                              PTh[:, 0:s.nk, s.col:s.col + P]))
                elif s.kind == "pv":
                    r = slice(64 * s.half, 64 * s.half + 64)
                    q = slice(s.q0, s.q0 + 256)
                    if s.na:
                        give(stt(T2[r, 0:256], ps[r, 0:256], 0.5, G2[r, s.pair % 2, q], ALU.mult, ALU.mult))
                        take()
                        done(rest(Ol[r, s.tile, q], T2[r, 0:256], Oh[r, s.tile, q]))
                    else:
                        take()
                        done(rest(Hl[r, s.tile, q], ps[r, 0:256], Hh[r, s.tile, q]))
                elif s.kind == "spgate":
                    for n in range(s.nn):
                        for h in range(2):
                            r = slice(64 * h, 64 * h + 64)
                            c = (s.n0 + n) * P
                            ins = tt(T2[r, c:c + P], ps[r, n * 256 + h * P:n * 256 + h * P + P], BS[r, s.m, :], ALU.add)
                    done(ins)
                elif s.kind == "gsplit":
                    give(stt(T2[:, 0:t], T2[:, 0:t], 0.5, SU[:, s.m, 0:t], ALU.mult, ALU.mult))
                    take()
                    done(rest(Hl[:, 6 + s.m, 0:t], T2[:, 0:t], Hh[:, 6 + s.m, 0:t]))
                elif s.kind == "four2":
                    take()
                    for lo, sz in segs(t):
                        ins = rest(Hl[:, 4 + s.m, lo:lo + sz], ps[:, lo:lo + sz], Hh[:, 4 + s.m, lo:lo + sz], four_scale(sz))
                    done(ins)
                elif s.kind == "unit":
                    m = s.m
                    if s.ev == "gate":
                        take()
                        done(stt(G[:, m, 0:t], T1[:, 0:t], 1.0, ps[:, 0:t], ALU.add, ALU.mult))
                    elif s.ev == "g":
                        take()
                        done(stt(G2[:, s.pair % 2, :], T1[:, 0:t], 1.0, ps[:, 0:t], ALU.add, ALU.mult))
                    elif s.ev == "cgate":
                        take()
                        chain(stt(T2[:, 0:t], T1[:, 0:t], 1.0, ps[:, 0:t], ALU.add, ALU.mult))
                        give(tt(T2[:, 0:t], T2[:, 0:t], T4[:, 0:t], ALU.mult))
                        take()
                        done(rest(Ol[:, m, :], T2[:, 0:t], Oh[:, m, :]))
                    elif s.ev == "poolmix":
                        give(stt(T2[:, 0:t], ps[:, 0:t], PSC[:, s.layer, m:m + 1], G[:, m, 0:t], ALU.mult, ALU.mult))
                        take()
                        done(rest(Hl[:, m, 0:t], T2[:, 0:t], Hh[:, m, 0:t]))
                    elif s.ev == "xupd":
                        for c, (lo, sz) in enumerate(segs(t)):
                            ins = stt(xseg(lo, m), ps[:, lo:lo + sz], MOD[:, s.sect, c, m:m + 1], xseg(lo, m), ALU.mult, ALU.add)
                        if s.nxT:
                            give(ins)
                            take()
                            ins = sum_squares(m, segs(s.nxT))
                        done(ins)
                    elif s.ev in ("q", "k"):
                        take()
                        hi, lo = (Qh, Ql) if s.ev == "q" else (Kh, Kl)
                        p = s.pair % 2
                        done(rest(lo[:, p, 0:t], ps[:, 0:t], hi[:, p, 0:t], 0.125 if s.ev == "q" else None))
                    elif s.ev == "cv":
                        if m == 0:
                            dve.memset(Z[:, 0:TX + 2:TX + 1], 0.0)
                        chain(tt(Z[:, 1:TX + 1], ps[:, 0:TX], T3[:, 0:TX], ALU.mult))
                        chain(dve.tensor_scalar(T4[:, 0:TX], Z[:, 0:TX], CW[:, 0, m:m + 1], CW[:, 3, m:m + 1], ALU.mult, ALU.add))
                        chain(stt(T4[:, 0:TX], Z[:, 1:TX + 1], CW[:, 1, m:m + 1], T4[:, 0:TX], ALU.mult, ALU.add))
                        done(stt(T4[:, 0:TX], Z[:, 2:TX + 2], CW[:, 2, m:m + 1], T4[:, 0:TX], ALU.mult, ALU.add))
                    elif s.ev == "cb":
                        done(stt(T4[:, 0:TX], ps[:, 0:TX], 0.5, T4[:, 0:TX], ALU.mult, ALU.mult))
                    elif s.ev in ("su", "sgv"):
                        take()
                        chain(dve.tensor_scalar(T2[:, 0:t], T1[:, 0:t], GELU_A, 1.0, ALU.mult, ALU.add))
                        give(tt(T2[:, 0:t], T2[:, 0:t], ps[:, 0:t], ALU.mult))
                        take()
                        if s.ev == "su":
                            done(stt(SU[:, m, 0:t], T1[:, 0:t], 1.0, ps[:, 0:t], ALU.add, ALU.mult))
                        else:
                            chain(stt(GV[:, m, 0:t], T1[:, 0:t], 1.0, ps[:, 0:t], ALU.add, ALU.mult))
                            done(stt(T2[:, 0:t], GV[:, m, 0:t], 0.25, GV[:, m, 0:t], ALU.mult, ALU.mult))
                    elif s.ev == "mlp":
                        take()
                        chain(tt(T2[:, 0:t], T1[:, 0:t], T1[:, 0:t], ALU.mult))
                        done(rest(Ml[:, m, 0:t], T2[:, 0:t], Mh[:, m, 0:t]))
                if s.ada and s.d1:
                    dve.wait_ge(dve_done, s.d1)
                for sect, k in s.ada:
                    ada_chunk(sect, k)


def four_scale(n):
    return float(1.0 / np.sqrt(n * 64.0))


def unit_columns(w, cols):
    return np.ascontiguousarray(w[:, cols].reshape(-1, P, len(cols)).transpose(1, 0, 2)).reshape(P, -1)


def constants():
    c = {}
    eye = np.eye(P, dtype=np.float32)
    c["ident"], c["ones"] = eye, np.ones((P, P), np.float32)
    c["bones"] = np.kron(np.eye(2), np.ones((64, 64))).astype(np.float32)
    swap = np.arange(P) ^ 16
    c["perm"] = eye[swap]
    hot = np.zeros((32, GRID_W, GRID_W), np.float32)
    for q in range(GRID_W):
        first = min(max(q - WIN // 2, 0), GRID_W - WIN)
        for j in range(GRID_W):
            if first <= j < first + WIN:
                hot[j - q + WIN - 1, q, j] = 1.0
            else:
                hot[NDC, q, j] = MASKED
    c["onehot"] = hot.reshape(32, -1)
    n = np.arange(64)
    a = 2 * np.pi * ((n[:, None] * n) % 64) / 64
    c["dft64"] = np.concatenate([np.kron(np.eye(2), np.cos(a)), np.kron(np.eye(2), np.sin(a))], 1).astype(np.float32)
    n = np.arange(TX)
    a = 2 * np.pi * ((n[:, None] * n) % TX) / TX
    c["dft_cos"] = np.cos(a).reshape(4, P, TX).transpose(1, 0, 2).astype(np.float32)
    c["dft_sin"] = (-np.sin(a)).reshape(4, P, TX).transpose(1, 0, 2).astype(np.float32)
    edge = np.zeros((P, 4, 2, PADL), np.float32)
    for g, w in enumerate(WINDOWS):
        for j in range(PADL):
            for side, (i, size) in enumerate(((j, TX), (TX - PADL + j, TX))):
                edge[:, g, side, j] = w / (min(i + w // 2, size) - max(i - w // 2, 0))
    c["edge"] = edge
    inv = np.float32(10000.0) ** (-np.arange(0, 32, 2, dtype=np.float32) / np.float32(32))
    tok = np.arange(TX)
    cos, sin = np.zeros((P, TX), np.float32), np.zeros((P, TX), np.float32)
    for p in range(P):
        f = p % 64
        pos = (tok // GRID_W if f < 32 else tok % GRID_W).astype(np.float32)
        ang = (pos * inv[f % 16]).astype(np.float32)
        cos[p] = np.cos(ang)
        sin[p] = np.sin(ang) * (-1 if f % 32 < 16 else 1)
    c["rope_cos"], c["rope_sin"] = cos, sin
    return c


def layout(i):
    i = {k: np.asarray(v) for k, v in i.items()}
    a = constants()
    a["xT"] = np.ascontiguousarray(i["x"][0].T)
    a["ctxT"] = np.ascontiguousarray(i["ctx"][0].T)
    a["ctxT_2"] = np.ascontiguousarray(i["ctx_2"][0].T)
    col = lambda v: np.ascontiguousarray(np.asarray(v).reshape(-1, P).T)
    a["cond"] = np.stack([col(i["c"][0]), col(i["c_ctx"]), col(i["c_2"][0]), col(i["c_ctx_2"])], 1)
    units = []

    def cols(w, m0, n=P):
        units.append(unit_columns(w, np.arange(m0, m0 + n)))

    def pool_units(j):
        for m in range(16):
            cols(i["pool_w_in"][j], m * P)
        grp = i["pool_w_grp"][j]
        for half in range(2):
            units.append(np.concatenate([unit_columns(grp[m // 2], np.arange(m % 2 * P, m % 2 * P + P))
                                         for m in range(half * 4, half * 4 + 4)], 1))
        for m in range(8):
            cols(i["pool_w_out"][j], m * P)

    pool_units(0)
    w = i["na_w_in"][0]
    for t in range(8):
        for part in (0, 1, 3, 2):
            cols(w, part * D + t * P)
    for m in range(8):
        cols(i["na_w_out"][0], m * P)
    w = i["conv_w_in"][0]
    for t in range(8):
        for part in (1, 2, 0, 3):
            cols(w, part * D + t * P)
    for m in range(8):
        cols(i["conv_w_out"][0], m * P)
    pool_units(1)
    for L in range(2):
        w = i["w_in_2"][L]
        cols(w, 512)
        pairs = [np.concatenate([np.arange(m * 64, m * 64 + 64), np.arange((m + 4) * 64, (m + 4) * 64 + 64)]) for m in range(4)]
        for m in range(4):
            units.append(unit_columns(w, pairs[m]))
        cols(w, 640)
        for m in range(6):
            cols(w, 768 + m * P)
        wo = i["w_out_2"][L][np.concatenate(pairs + [np.arange(512, 1024)])]
        for m in range(8):
            cols(wo, m * P)
        for c in range(4):
            for m in range(8):
                cols(i["w_mlp1_2"][L], c * D + m * P)
            for m in range(8):
                cols(i["w_mlp2_2"][L][c * D:c * D + D], m * P)
    a["wpack"] = np.stack(units)
    ada = [i["ada_w"][L][:, s * D:s * D + D] for L in range(4) for s in range(3)]
    ada += [i["w_ada_2"][L][:, s * D:s * D + D] for L in range(2) for s in range(6)]
    a["adapack"] = np.concatenate([x.reshape(8, P, D) for x in ada])
    bias = [i["ada_b"][L][s * D:s * D + D] for L in range(4) for s in range(3)]
    bias += [i["b_ada_2"][L][s * D:s * D + D] for L in range(2) for s in range(6)]
    a["adab"] = np.stack([col(x) for x in bias], 1)
    gains = [*i["norm_g"], *i["norm1_g_2"], *i["norm2_g_2"], i["final_g"]]
    a["normg"] = np.stack([col(x) for x in gains], 1)
    a["psc"] = np.stack([col(x) for x in i["pool_scale"]], 1)
    a["cw"] = np.stack([col(x) for x in [*i["conv_dw"][0], i["conv_db"][0]]], 1)
    twice = lambda v: np.concatenate([v, v])
    a["hg"] = np.stack([np.stack([twice(i["q_norm_g_2"][L]), twice(i["k_norm_g_2"][L]), i["gmlp_v_g_2"][L][:P],
                                  i["gmlp_v_g_2"][L][P:]], 1) for L in range(2)], 1)
    rpb = np.ones((32, 240), np.float32)
    rpb[:NDC] = i["na_rpb"][0].reshape(240, NDC).T
    a["rpb"] = rpb
    a["wsp"] = np.ascontiguousarray(i["w_spatial_2"].transpose(0, 3, 1, 2)).reshape(2, P, 512)
    bs = i["b_spatial_2"].reshape(2, 2, 2, 1, P)
    a["bsp"] = np.ascontiguousarray(np.broadcast_to(bs, (2, 2, 2, 64, P)).transpose(0, 2, 3, 1, 4)).reshape(2, P, 2, P)
    return {k: np.ascontiguousarray(v) for k, v in a.items()}


def kernel(**inputs):
    import concourse.bacc as bacc
    from concourse.bass_utils import run_bass_kernel_spmd

    arrays = layout(inputs)
    nc = bacc.Bacc("TRN2", target_bir_lowering=False, num_devices=1)
    aps = {k: nc.dram_tensor("in_" + k, v.shape, mybir.dt.from_np(v.dtype), kind="ExternalInput").ap()
           for k, v in arrays.items()}
    out = nc.dram_tensor("out_xT", (D, TX), F32, kind="ExternalOutput").ap()
    build_blocks(nc, aps, out)
    r = run_bass_kernel_spmd(nc, [{"in_" + k: v for k, v in arrays.items()}], core_ids=[0])
    return r.results[0]["out_xT"].T[None]
```

```python
from contextlib import ExitStack

import numpy as np
from concourse import mybir

P = 128
D = 1024
KT = D // P
TX, TC = 512, 256
TT = TX + TC
NT = TT // P
EPS = 1e-6
F32 = mybir.dt.float32
F32R = mybir.dt.float32r
ALU = mybir.AluOpType
ACT = mybir.ActivationFunctionType
AX = mybir.AxisListType
GRID_W, ROWS, WIN = 64, 8, 16
NDR = 2 * 8 - 1
NDC = 2 * WIN - 1
NHEADS_NA = 16
PADL = 8
UX, UC = 0, TX + 2 * PADL
UW = TX + TC + 4 * PADL
WINDOWS = (2, 4, 8, 16)
MASKED = -1e30
N_SECT = 24
GELU_C = 0.7978845608028654
GELU_A = 0.044715
SECT0 = [0, 3, 6, 9, 12, 18]
ON_DVE = 6
CTX_SECT = {0, 1, 2, 3, 4} | set(range(12, 18)) | {18, 19}


class Step:

    def __init__(self, kind, T=None, m=None, src=None, ev=None, part=None, pair=None, grp=None, layer=None, sect=None,
                 nxT=0, k=None, g=None, c=None, x0=None, what=None, half=None, qt=None, st=None, eb=None, nk=None,
                 first=False, na=False, col=None, tile=None, q0=None, n0=None, nn=None, in_end=None, has_turn=False, late=False,
                 after=()):
        self.kind, self.T, self.m, self.src, self.ev, self.part, self.pair = kind, T, m, src, ev, part, pair
        self.grp, self.layer, self.sect, self.nxT, self.k, self.g, self.c = grp, layer, sect, nxT, k, g, c
        self.x0, self.what, self.half, self.qt, self.st, self.eb, self.nk = x0, what, half, qt, st, eb, nk
        self.first, self.na, self.col, self.tile, self.q0, self.n0, self.nn = first, na, col, tile, q0, n0, nn
        self.in_end, self.has_turn, self.after, self.late = in_end, has_turn, list(after), late
        self.turn, self.w, self.ada = None, None, []
        self.pt, self.reader, self.scores, self.trans, self.of, self.in_turn = 0, self, None, None, None, False
        self.partner, self.joined, self.back, self.fill = None, False, None, 0
        self.idle = 0


ACT_ONLY, DVE_ONLY = {"u", "v", "cg", "sk", "sq", "sf"}, {"cv", "cb"}


def ends_in(s):
    if s.kind in ("upart", "scores", "trans", "pvmm", "back"):
        return None
    if s.kind == "bias_row":
        return "row"
    if s.kind in ("gtrans", "four1") or (s.kind == "unit" and s.ev in ACT_ONLY):
        return "act"
    return "dve"


def plan():
    steps = []
    ada_queue = [(s, k) for s in range(N_SECT) for k in range(KT)]
    waiting_red = []
    rows = []
    results = []

    def add(kind, **a):
        s = Step(kind, **a)
        s.i = len(steps)
        steps.append(s)
        return s

    owed = [0]

    def with_ada(s, n=1):
        owed[0] += n
        for _ in range(min(2, owed[0]) if n else 0):
            if ada_queue and not (s.ada and s.ada[-1][1] == KT - 1):
                s.ada.append(ada_queue.pop(0))
                owed[0] -= 1

    def ada_red(now=False):
        while waiting_red and (now or waiting_red[0][0] < len(steps) - 1):
            add("adared", sect=waiting_red.pop(0)[1], has_turn=True)

    def half_unit(src, ev, T, part, m=0, **a):
        return add("unit" if part else "upart", src=src, ev=ev, T=T, m=m, part=part, has_turn=True, **a)

    def full(src, ev, T, m=0, after=(), chunks=1, **a):
        s = add("unit", src=src, ev=ev, T=T, m=m, part=None, has_turn=True, **a)
        s.after = list(after)
        if ev == "xupd" and m == KT - 1:
            owed[0] += 1
            chunks = 0
        with_ada(s, chunks)
        if s.ada and s.ada[-1][1] == KT - 1:
            waiting_red.append((s.i, s.ada[-1][0]))
        ada_red()
        return s

    add("silu_c")
    for k in range(KT):
        add("sq0", k=k, T=TT, x0=0)

    first = add("adafirst")
    add("adape", sect=0, has_turn=True)
    del ada_queue[:2 * KT]

    def norm(T, g, sect):
        if g:
            ada_red(True)
            add("gain", g=g, T=T, sect=sect)
        add("nstat", T=T, g=g, sect=sect, has_turn=True)
        if g == 0:
            add("adared", sect=1, has_turn=True).after = [first]
        back = add("back", T=T)
        if g == 0:
            add("gain", g=g, T=T, sect=sect)
        tiles = [add("ntile", T=T, k=k, g=g, sect=sect) for k in range(KT)]
        back.reader, tiles[0].back = tiles[-1], back
        return tiles

    def join(u, v):
        u.partner, v.joined = v, True

    def pool_layer(L, T, nxT):
        tiles = norm(T, L, SECT0[L])
        d = []
        us = []
        for m in range(KT):
            us.append(full("H", "u", T, m, after=tiles if m < 2 else ()))
            d.append(add("pool", T=T, m=m))
        join(us[0], us[1])
        for m in range(KT):
            full("H", "gate", T, m, chunks=2 if L == 0 and m < 4 else 1)
            if L == 3:
                add("sq0", k=m, T=TC, x0=TX)
        y = []
        for half in range(2):
            for mm in range(4):
                m = half * 4 + mm
                s = add("unit", src="D", ev="poolmix", T=T, m=m, part=None, grp=mm, layer=L // 3, has_turn=True)
                s.after = d[-1:]
                y.append(s)
                if L == 0:
                    for _ in range((0, 2, 2, 2, 2, 2, 3, 3)[m]):
                        add("bias_row", g=len(rows) // 8, c=len(rows) % 8, st=len(rows) % 2, k=len(rows) + 1)
                        rows.append(1)
        for m in range(KT):
            full("H", "xupd", T, m, after=y if m == 0 else (), sect=SECT0[L] + 2, nxT=nxT)

    pool_layer(0, TT, TT)

    tiles = norm(TT, 1, SECT0[1])
    seq = ["q", "k", "g", "v"]
    made = {}

    def first_of_pair(j, e):
        made[e] = full("H", e, TT if e in "kv" else TX, 0, after=tiles if j < 2 else (), pair=0)

    for j, e in enumerate(seq[:3]):
        first_of_pair(j, e)
    join(made["q"], made["k"])
    n_steps = KT * 8
    sc, tr, pv, soft = {}, {}, {}, {}

    def na_scores(n, q, k):
        sc[n] = add("scores", na=True, pair=n // 8, half=n % 8 // 4, qt=n % 4, st=0, eb=n % 2, first=n % 4 == 0, nk=NT)
        sc[n].after = [q, k]

    def na_trans(n):
        tr[n] = add("trans", na=True, eb=n % 2, col=n % 2 * P, nk=NT, qt=n % 4)
        tr[n].after = [soft[n - 1]]
        tr[n].idle = n >= n_steps - 8

    def na_soft(n):
        soft[n] = add("soft", na=True)
        soft[n].scores, soft[n].trans = sc.get(n + 1), tr.get(n)
        for x in (soft[n].scores, soft[n].trans):
            if x is not None:
                x.reader = soft[n]

    def na_pv(n):
        mm = add("pvmm", nk=NT, has_turn=True)
        mm.after = [soft[n + 1], vt]
        return mm

    def na_pv_out(n, mm):
        pv[n] = mm.reader = add("pv", na=True, pair=n // 8, tile=n // 8, half=n % 8 // 4, q0=n % 4 * P)
        pv[n].of = mm

    na_scores(0, made["q"], made["k"])
    na_soft(-1)
    first_of_pair(3, "v")
    vt = add("vtrans")
    vt.after = [made["v"]]
    for n in range(n_steps):
        t, i = n // 8, n % 8
        if i == 0:
            cur = {}
        if n + 1 < n_steps:
            src = cur if i == 7 else made
            na_scores(n + 1, src["q"], src["k"])
        if n % 2 == 0 and n:
            mm = na_pv(n - 2)
        na_trans(n)
        if i % 2 == 0 and t + 1 < KT:
            half_unit("H", seq[i // 2], TT if seq[i // 2] in "kv" else TX, 0, pair=t + 1)
        na_soft(n)
        if n % 2 == 0 and n:
            na_pv_out(n - 2, mm)
        if i % 2 and t + 1 < KT:
            e = seq[i // 2]
            cur[e] = u = half_unit("H", e, TT if e in "kv" else TX, 1, pair=t + 1)
            with_ada(u)
            if u.ada and u.ada[-1][1] == KT - 1:
                waiting_red.append((u.i, u.ada[-1][0]))
        if i == 0 and t:
            vt = add("vtrans")
            vt.after = [made["v"]]
        if i % 2:
            ada_red()
        if i == 7:
            made = cur or made
    na_pv_out(n_steps - 2, na_pv(n_steps - 2))
    tile_of = [pv[8 * t + 6] for t in range(KT)]
    for m in range(KT):
        full("O", "xupd", TX, m, after=tile_of if m == 0 else (), sect=SECT0[1] + 2, nxT=TX)

    tiles = norm(TX, 2, SECT0[2])
    y = []
    for m in range(KT):
        for j, e in enumerate(["cg", "cv", "cb", "cgate"]):
            u = full("H", e, TX, m, after=tiles if m == 0 and j < 2 else ())
            if m == 0 and j == 1:
                join(before, u)
            before = u
        y.append(u)
    for m in range(KT):
        full("O", "xupd", TX, m, after=y if m == 0 else (), sect=SECT0[2] + 2, nxT=TX)

    pool_layer(3, TX, TX)
    add("nstat", T=TX, g=None, sect=None, has_turn=True)
    back = add("back", T=TX)
    for k in range(KT):
        back.reader = add("final", k=k, T=TX)
        back.reader.back = back

    for L in range(2):
        both = L == 0
        T = TT if both else TX
        sect = SECT0[4 + L]
        tiles = norm(TT, 4 + L, sect)
        todo, rp = None, None

        def head_steps(u):
            kind, m, t = u.what, u.m, u.T
            hn = add("hnorm", T=t, what=kind, m=m, layer=L, st=0)
            hn.after = [u]
            back = add("back", T=t)
            if kind == "sgv":
                back.reader = add("gnorm", T=t, m=m, layer=L)
            else:
                back.reader = add("rope", T=t, what=kind, m=m, layer=L, st=1)
            back.reader.back = back
            return back.reader

        units = [("sk", 0, TT)] + [("sq", m, T) for m in range(4)] + [("v", 0, TT)]
        units += [("sf", 0, T), ("sf", 1, T), ("su", 0, T), ("su", 1, T), ("sgv", 0, T), ("sgv", 1, T)]
        hn_of = {}
        for j, (e, m, t) in enumerate(units):
            if j < 2:
                u = full("H", e, t, m, after=tiles, layer=L, what=e)
                if j:
                    join(sk, u)
                else:
                    sk = u
                    hn_of["sk", 0] = head_steps(u)
            else:
                first = half_unit("H", e, t, 0, m=m)
                if todo is not None:
                    hn_of[todo.what, todo.m] = head_steps(todo)
                if e == "sf" and m == 0:
                    vt = add("vtrans")
                    vt.after = [v]
                u = half_unit("H", e, t, 1, m=m, layer=L, what=e, pair=0)
                with_ada(u)
                if u.ada and u.ada[-1][1] == KT - 1:
                    waiting_red.append((u.i, u.ada[-1][0]))
                ada_red()
            if e == "v":
                v = u
            todo = u if e in ("sq", "sgv") else None
        last_in = u
        qk = hn_of["sq", 3]
        nts = T // P
        four = [(m, n0) for m in range(2) for n0 in range(0, nts, 4)]
        ab = []

        def four1():
            if four:
                m, n0 = four.pop(0)
                ab.append(add("four1", m=m, n0=n0, nn=min(4, nts - n0), has_turn=True, in_end=last_in))

        four1()
        hn = add("hnorm", T=last_in.T, what="sgv", m=1, layer=L, st=0)
        hn.after = [last_in]
        gt, gsp = {}, {}

        def gtrans(m):
            gt[m] = add("gtrans", T=T, m=m, has_turn=True)
            gt[m].after = [hn_of["sgv", m]]

        def spgate(m):
            for n0 in range(0, nts, 4):
                add("spgate", T=T, m=m, n0=n0, nn=min(4, nts - n0), layer=L, has_turn=True).after = [gt[m]]

        gtrans(0)
        back = add("back", T=T)
        four1()
        back.reader = hn_of["sgv", 1] = add("gnorm", T=T, m=1, layer=L)
        back.reader.back = back
        spgate(0)
        gtrans(1)
        gsp[0] = add("gsplit", T=T, m=0)
        while four:
            four1()
        spgate(1)
        gsp[1] = add("gsplit", T=T, m=1)
        todo = []
        for m in range(4):
            for half in range(2):
                for qt in range(4):
                    todo.append((m, half, qt, NT))
                if both:
                    for qt in range(4, 6):
                        todo.append((m, half, qt, 2))
        sc, tr, pv_of, soft = {}, {}, {}, {}

        def s_soft(n):
            soft[n] = add("soft", na=False)
            soft[n].scores, soft[n].trans = sc.get(n + 2), tr.get(n)
            for x in (soft[n].scores, soft[n].trans):
                if x is not None:
                    x.reader = soft[n]

        def s_scores(n):
            if n < len(todo):
                m, half, qt, nk = todo[n]
                sc[n] = add("scores", na=False, pair=m, half=half, qt=qt, st=n % 2, eb=n % 2, nk=nk)
                sc[n].after = [qk]

        def s_pv(n):
            mm = add("pvmm", nk=todo[n][3])
            mm.pt = n // 2 % 2
            mm.after = [soft[n + 1], vt]
            return mm

        def s_pv_out(n, of):
            m, half, qt, nk = todo[n]
            pv_of[m] = of.reader = add("pv", na=False, pair=m, tile=m, half=half, q0=qt * P)
            pv_of[m].of = of

        mix = []
        for m in range(2):
            s_scores(m)
            s_soft(m - 2)
            s = add("four2", m=m, T=T, has_turn=True)
            s.after = ab
            mix.append(s)
        for n in range(len(todo)):
            s_scores(n + 2)
            if n % 2 == 0 and n >= 4:
                s_pv(n - 4).in_turn = True
            tr[n] = add("trans", na=False, eb=n % 2, col=n % 2 * P, nk=todo[n][3], has_turn=True, qt=todo[n][2])
            tr[n].pt = n // 2 % 2
            tr[n].in_turn = n % 2 == 0 and n >= 4
            tr[n].after = [soft[n - 2]]
            s_soft(n)
            if n % 2 == 0 and n >= 4:
                s_pv_out(n - 4, tr[n])
        for n in (len(todo) - 4, len(todo) - 2):
            mm = s_pv(n)
            mm.has_turn = True
            s_pv_out(n, mm)
        ready = [pv_of[0], pv_of[1], pv_of[2], pv_of[3], mix[0], mix[1], gsp[0], gsp[1]]
        for m in range(KT):
            full("H", "xupd", T, m, after=ready if m == 0 else (), sect=sect + 2, nxT=T, late=m == 0)
        tiles = norm(T, 6 + L, sect + 3)
        for c in range(4):
            hid = [full("H", "mlp", T, m, after=tiles if c == 0 and m < 2 else ()) for m in range(KT)]
            if c == 0:
                join(hid[0], hid[1])
            for m in range(KT):
                s = full("M", "xupd", T, m, after=hid if m == 0 else (), sect=sect + 5, nxT=T if c == 3 and L == 0 else 0)
                if c == 3 and L == 1:
                    results.append(s)
    turn, w = 0, 0
    for s in steps:
        if s.kind == "upart":
            s.turn, s.w = turn, w
        elif s.kind == "unit":
            if s.ev == "poolmix":
                s.w = w
                if s.grp == 3:
                    w += 1
            else:
                s.w = w
                w += 1
            s.turn = turn
            turn += 1
        elif s.has_turn:
            s.turn = turn
            turn += 1
        elif s.idle:
            s.idle = turn
        elif s.in_turn:
            s.turn = turn
        elif s.of is not None:
            s.turn = s.of.turn
    fills = [0, 0]
    for s in steps:
        n = {"hnorm": 0, "back": 0, "rope": 1, "vtrans": 1, "scores": s.st, "bias_row": s.st, "trans": 1 if s.na else None}.get(s.kind)
        if n is not None:
            fills[n] += 1
            s.fill = fills[n]
    a = d = 0
    for s in steps:
        s.a0, s.d0 = a, d
        a += ends_in(s) == "act"
        d += ends_in(s) == "dve"
        s.a1, s.d1 = a, d
    return steps, w, results




def build_blocks(nc, A, out):
    steps, n_units, results = plan()
    with ExitStack() as ctx:
        at = [16512]

        def sb(name, shape, dt=F32, offset=None):
            size = int(np.prod(shape[1:])) * 4
            if offset is None:
                offset = at[0]
                at[0] += (size + 31) // 32 * 32
            return nc.alloc_sbuf_tensor_at(name, list(shape), dt, offset=offset)

        Xx = sb("x_lat", [P, KT, TX])
        xc_at = at[0]
        Xc = sb("x_ctx", [P, KT, TC])
        h_at = at[0]
        Hh, Hl = sb("h_hi", [P, KT, TT], F32R), sb("h_lo", [P, KT, TT], F32R)
        RAW = sb("w_raw", [P, 2, D])
        Wh, Wl = sb("w_hi", [P, 2, D], F32R), sb("w_lo", [P, 2, D], F32R)
        ADR = sb("ada_raw", [P, 2, D])
        ACC = sb("ada_acc", [P, 2, D])
        T = []
        t_at = []
        for n in range(4):
            t_at.append(at[0])
            T.append(sb(f"tmp{n + 1}", [P, UW]))
        T1, T2, T3, T4 = T
        IDN, ONES, BONES, PERM = (sb(n, [P, P]) for n in ("ident", "ones", "head_ones", "rope_swap"))
        CS = sb("dft64", [P, 2 * P])
        MOD = sb("modulation", [P, N_SECT, 2, KT])
        ADAB = sb("ada_bias", [P, N_SECT, KT])
        NG = sb("norm_gains", [P, 9, KT])
        CV, CVT, SC = sb("cond", [P, 4, KT]), sb("cond_tanh", [P, 4, KT]), sb("cond_silu", [P, 4, KT])
        PSC = sb("pool_scale", [P, 2, KT])
        CW = sb("conv_cols", [P, 4, KT])
        HG = sb("head_gains", [P, 2, 4])
        EDGE = sb("pool_edges", [P, 4, 2, PADL])
        GA = sb("gain_cols", [P, 2, KT])
        ST = sb("softmax_stats", [P, 2, 8])
        EPSC, SQT = sb("eps", [P, 1]), sb("sqrt_tmp", [P, 1])
        RMS = sb("rms", [P, 2 * NT])
        ar = at[0]

        def arena(name, shape, dt, off):
            return sb(name, shape, dt, ar + off)

        K1 = 1024
        HOT, RPB = sb("onehot", [96, 1536], F32, t_at[2]), sb("rpb", [96, 240], F32, t_at[0] + 2048)
        STAGE = [sb("bias_out0", [P, 512], F32, t_at[0]), arena("bias_out1", [P, 512], F32, 72 * K1)]
        Dh, Dl = arena("d_hi", [P, KT, TT], F32R, 0), arena("d_lo", [P, KT, TT], F32R, 24 * K1)
        G, U = arena("gate", [P, KT, TT], F32, 48 * K1), arena("u_padded", [P, UW], F32, 72 * K1)
        Oh, Ol = arena("o_hi", [P, KT, TX], F32R, 0), arena("o_lo", [P, KT, TX], F32R, 16 * K1)
        PTh, PTl = [arena("pt_hi0", [P, NT, 256], F32R, 32 * K1)], [arena("pt_lo0", [P, NT, 256], F32R, 38 * K1)]
        Qh, Ql = arena("q_hi", [P, 2, TX], F32R, 44 * K1), arena("q_lo", [P, 2, TX], F32R, 48 * K1)
        Kh, Kl = arena("k_hi", [P, 2, TT], F32R, 52 * K1), arena("k_lo", [P, 2, TT], F32R, 58 * K1)
        Vh, Vl = arena("v_hi", [P, NT, P], F32R, 64 * K1), arena("v_lo", [P, NT, P], F32R, 67 * K1)
        G2 = arena("na_gate", [P, 2, TX], F32, 70 * K1)
        BIAS = [sb(f"bias{n}", [P, 14 * GRID_W], F32, xc_at + n * 3584) for n in range(2)]
        Z = arena("conv_in", [P, TX + 2], F32, 70 * K1)
        SQh, SQl = arena("sq_hi", [P, 4, TT], F32R, 0), arena("sq_lo", [P, 4, TT], F32R, 12 * K1)
        SKh, SKl = arena("sk_hi", [P, TT], F32R, 24 * K1), arena("sk_lo", [P, TT], F32R, 27 * K1)
        F = arena("fourier_in", [P, 2, TT], F32, 44 * K1)
        SU = arena("gmlp_u", [P, 2, TT], F32, 50 * K1)
        GV = arena("gmlp_v", [P, 2, TT], F32, 56 * K1)
        PTh.append(arena("pt_hi1", [P, NT, 256], F32R, 44 * K1))
        PTl.append(arena("pt_lo1", [P, NT, 256], F32R, 50 * K1))
        GT = [x[:, 0:TT].rearrange("p (n f) -> p n f", f=P) for x in (T1, T3)]
        AB = arena("fourier_mid", [P, NT, 2, 256], F32, 32 * K1)
        ROPC, ROPS = arena("rope_cos", [P, TX], F32, 70 * K1), arena("rope_sin", [P, TX], F32, 72 * K1)
        WS, BS = arena("w_spatial", [P, 512], F32, 74 * K1), arena("b_spatial", [P, 2, P], F32, 30 * K1)
        DC = sb("dft_cos", [P, 4, TX], F32, h_at)
        DS = sb("dft_sin", [P, 4, TX], F32, h_at + KT * TT * 4)
        Mh, Ml = arena("m_hi", [P, KT, TT], F32R, 0), arena("m_lo", [P, KT, TT], F32R, 24 * K1)
        EX, DIAG = [T4, T2], sb("softmax_diag", [P, 2, P], F32, t_at[0])
        PVT = sb("pv_tmp", [P, 256], F32, xc_at + 7168)
        adx_a, adx_b = arena("ada_first_a", [P, 12, D], F32, 0), sb("ada_first_b", [P, 4, D], F32, h_at)
        ADX = [adx_a[:, n] if n < 12 else adx_b[:, n - 12] for n in range(2 * KT)]
        bias_d = nc.dram_tensor("bias_table", [240, GRID_W, GRID_W], F32, kind="Internal").ap()

        PS = ctx.enter_context(nc.psum_tensor("turns", [P, 2, 1024], F32))
        SP_ = ctx.enter_context(nc.psum_tensor("scores", [P, 2, 1024], F32))

        def sem(name):
            return ctx.enter_context(nc.semaphore(name))

        raw_landed = [sem(f"raw_landed{n}") for n in range(2)]
        w_rounded, w_split = sem("w_rounded"), sem("w_split")
        ada_landed = [sem(f"ada_landed{n}") for n in range(2)]
        ada_done = sem("ada_done")
        cond_in, rows_done = sem("cond_in"), sem("rows_done")
        adx_in = [sem(f"ada_first_in{n}") for n in range(2 * KT)]
        turn_mm = sem("turn_mm")
        score_mm = [sem(f"score_mm{n}") for n in range(2)]
        act_done, dve_done = sem("act_done"), sem("dve_done")
        for_dve, for_act = sem("piece_for_dve"), sem("piece_for_act")
        act_own, dve_own = sem("act_own"), sem("dve_own")
        consts_in, x_in, hot_in = sem("consts_in"), sem("x_in"), sem("hot_in")
        bias_out = [sem(f"bias_out{n}") for n in range(2)]
        bias_in = [sem(f"bias_in{n}") for n in range(2)]
        ctx2_in, dft_in, sp_in, out_done = sem("ctx2_in"), sem("dft_in"), sem("sp_in"), sem("out_done")

        turn_of_w = {}
        for s in steps:
            if s.kind == "unit":
                turn_of_w[s.w] = s.turn
        red_turn = {s.sect: s.turn for s in steps if s.kind == "adared"}
        step_of_turn = {s.turn: s for s in steps if s.has_turn and s.kind != "upart"}
        by_kind = {}
        for s in steps:
            by_kind.setdefault(s.kind, []).append(s)
        na_scores = [s for s in by_kind["scores"] if s.na]
        heads_na = [na_scores[i * 4:i * 4 + 4] for i in range(NHEADS_NA)]
        na_pv_end = [s for s in by_kind["pv"] if s.na][-1]
        last_gate0 = [s for s in by_kind["unit"] if s.ev == "gate"][KT - 1]
        first_xupd = [s for s in by_kind["unit"] if s.ev == "xupd"][0]
        first_ctx2 = [s for s in by_kind["sq0"] if s.x0 == TX][0]
        na_norm_end = [s for s in by_kind["ntile"] if s.g == 1][-1]
        four_first = [s for s in by_kind["four1"] if s.m == 0 and s.n0 == 0]
        sk_steps = [s for s in by_kind["unit"] if s.ev == "sk"]

        def segs(t):
            return [(0, TX)] if t == TX else [(0, TX), (TX, TC)]

        def xseg(lo, m):
            return Xx[:, m, :] if lo == 0 else Xc[:, m, :]

        block = ctx.enter_context(nc.Block())

        @block.sync
        def _(sp):
            sp.dma_start(CV[:], A["cond"]).then_inc(cond_in, 16)
            sp.dma_start(Xx[:], A["xT"].rearrange("(k p) t -> p k t", p=P)).then_inc(x_in, 16)
            sp.dma_start(Xc[:], A["ctxT"].rearrange("(k p) t -> p k t", p=P)).then_inc(x_in, 16)
            for dst, src in ((ONES, "ones"), (IDN, "ident"), (BONES, "bones"), (PERM, "perm"), (CS, "dft64"), (ADAB, "adab"),
                             (NG, "normg"), (PSC, "psc"), (CW, "cw"), (HG, "hg"), (EDGE, "edge")):
                sp.dma_start(dst[:], A[src]).then_inc(consts_in, 16)
            for n in range(2 * KT):
                sp.dma_start(ADX[n], A["adapack"][n % 2 * KT + n // 2]).then_inc(adx_in[n], 16)
            for w in range(3):
                if w == 2:
                    sp.wait_ge(w_split, 1)
                sp.dma_start(RAW[:, w % 2, :], A["wpack"][w]).then_inc(raw_landed[w % 2], 16)
            chunk = 2 * KT
            for s in steps:
                for _ in s.ada:
                    if chunk >= 2 * KT + 2:
                        sp.wait_ge(ada_done, chunk - 1 - 2 * KT)
                    sp.dma_start(ADR[:, chunk % 2, :], A["adapack"][chunk]).then_inc(ada_landed[chunk % 2], 16)
                    chunk += 1
                if s.kind == "unit" and turn_of_w[s.w] == s.turn and s.w + 3 < n_units:
                    w = s.w + 3
                    sp.wait_ge(w_split, w - 1)
                    sp.dma_start(RAW[:, w % 2, :], A["wpack"][w]).then_inc(raw_landed[w % 2], 16)
                if s is last_gate0:
                    sp.wait_ge(dve_done, s.d1)
                    sp.dma_start(HOT[:], A["onehot"]).then_inc(hot_in, 16)
                    sp.dma_start(RPB[:], A["rpb"]).then_inc(hot_in, 16)
                if s is na_norm_end or (s.kind == "scores" and s.na and s.first):
                    if s is na_norm_end:
                        sp.wait_ge(dve_done, s.d1)
                        for n in range(2):
                            sp.wait_ge(bias_out[n], 16 * 8)
                        heads = [0]
                    else:
                        n = s.pair * 2 + s.half + 1
                        heads = [n] if n < NHEADS_NA else []
                        if n >= 2 and heads:
                            sp.wait_ge(dve_done, heads_na[n - 2][-1].reader.d1)
                    for n in heads:
                        for r in range(2):
                            sp.dma_start(BIAS[n % 2][r * 64:r * 64 + 64, :].rearrange("c (s j) -> c s j", j=GRID_W),
                                         bias_d[n * NDR + 1 - r:n * NDR + 15 - r].rearrange("s c j -> c s j")
                                         ).then_inc(bias_in[n % 2], 16)
                if s is first_ctx2:
                    sp.wait_ge(dve_done, na_pv_end.d1)
                    sp.dma_start(Xc[:], A["ctxT_2"].rearrange("(k p) t -> p k t", p=P)).then_inc(ctx2_in, 16)
                if s in sk_steps:
                    L = sk_steps.index(s)
                    sp.wait_ge(dve_done, s.after[0].d1)
                    sp.dma_start(ROPC[:], A["rope_cos"]).then_inc(sp_in, 16)
                    sp.dma_start(ROPS[:], A["rope_sin"]).then_inc(sp_in, 16)
                    sp.dma_start(WS[:], A["wsp"][L]).then_inc(sp_in, 16)
                    sp.dma_start(BS[:], A["bsp"][L]).then_inc(sp_in, 16)
                if s in four_first:
                    sp.wait_ge(turn_mm, s.in_end.turn + 1)
                    sp.dma_start(DC[:], A["dft_cos"]).then_inc(dft_in, 16)
                    sp.dma_start(DS[:], A["dft_sin"]).then_inc(dft_in, 16)
            for m, s in enumerate(results):
                sp.wait_ge(dve_done, s.d1)
                sp.dma_start(out[m * P:m * P + P, :], Xx[:, m, :]).then_inc(out_done, 16)
            sp.wait_ge(out_done, 16 * KT)

        @block.gpsimd
        def _(pool):
            for w in range(n_units):
                b = w % 2
                pool.wait_ge(w_rounded, w + 1)
                pool.tensor_tensor(Wl[:, b, :], RAW[:, b, :], Wh[:, b, :].bitcast(F32), ALU.subtract).then_inc(w_split, 1)

        @block.tensor
        def _(pe):
            def wait_steps(after):
                rows = max([x.k for x in after if x.kind == "bias_row"], default=0)
                if rows:
                    pe.wait_ge(rows_done, rows)
                a = max([x.a1 for x in after if ends_in(x) == "act"], default=0)
                d = max([x.d1 for x in after if ends_in(x) == "dve"], default=0)
                if a:
                    pe.wait_ge(act_done, a)
                if d:
                    pe.wait_ge(dve_done, d)

            def free_turn(s):
                if s.turn >= 2:
                    wait_steps([step_of_turn[s.turn - 2].reader])

            last_scores = [None, None]

            def free_scores(b, s):
                if last_scores[b] is not None:
                    wait_steps([last_scores[b].reader])
                last_scores[b] = s

            def keep_warm(n, turn=None):
                if turn is not None:
                    wait_steps([step_of_turn[turn - 2].reader])
                    dst = PS[:, turn % 2, 0:256]
                else:
                    if last_scores[1] is not None:
                        wait_steps([last_scores[1].reader])
                    dst = SP_[:, 1, 0:256]
                for _ in range(n):
                    pe.matmul(dst, ONES[:], CS[:], start=True, stop=True)

            src_of = {"H": (Hh, Hl), "O": (Oh, Ol), "M": (Mh, Ml), "D": (Dh, Dl)}

            def three_pass(dst, wh, wl, xh, xl, t, first, last):
                for n, (w, x) in enumerate(((wh, xh), (wh, xl), (wl, xh))):
                    for lo, sz in segs(t):
                        ins = pe.matmul(dst[:, lo:lo + sz], w, x[:, lo:lo + sz], start=first and n == 0,
                                        stop=last and n == 2)
                return ins

            def tile(s, k, first, last):
                if len(s.after) == KT:
                    wait_steps(s.after[k:k + 1])
                xh, xl = src_of[s.src]
                col = (s.grp * 2 + k if s.ev == "poolmix" else k) * P
                x = s.m // 2 * 2 + k if s.ev == "poolmix" else k
                ins = three_pass(PS[:, s.turn % 2, :], Wh[:, s.w % 2, col:col + P], Wl[:, s.w % 2, col:col + P],
                                 xh[:, x, :], xl[:, x, :], s.T, first and s.part != 1, last and s.part != 0)
                if last and s.part != 0:
                    ins.then_inc(turn_mm, 1)

            def unit(s):
                if s.joined:
                    return
                v = s.partner
                if v:
                    keep_warm(8)
                if s.ev == "poolmix" and s.T == TX:
                    keep_warm(3)
                for x in (s, v) if v else (s,):
                    if x.part != 1:
                        pe.wait_ge(w_split, x.w + 1)
                        free_turn(x)
                if s.after and len(s.after) < KT:
                    wait_steps(s.after)
                ks = list(range(KT))
                if s.part is not None:
                    ks = ks[s.part * 4:s.part * 4 + 4]
                if s.ev == "poolmix":
                    ks = [0, 1]
                if s.late:
                    ks = ks[4:] + ks[:4]
                lag = 2 if v else 0
                for j in range(len(ks) + lag):
                    if j < len(ks):
                        tile(s, ks[j], j == 0, j == len(ks) - 1)
                    if v and j >= lag:
                        tile(v, j - lag, j == lag, j == len(ks) + lag - 1)

            for s in steps:
                b = None if s.turn is None else s.turn % 2
                if s.kind in ("unit", "upart"):
                    unit(s)
                elif s.kind == "bias_row":
                    if s.g == 0 and s.c == 0:
                        pe.wait_ge(hot_in, 32)
                    free_scores(s.st, s)
                    r, c = slice(s.c // 3 * 32, s.c // 3 * 32 + 32), s.c % 3 * 512
                    pe.matmul(SP_[0:120, s.st, 0:512], RPB[r, s.g * 120:s.g * 120 + 120], HOT[r, c:c + 512],
                              start=True, stop=True).then_inc(score_mm[s.st], 1)
                elif s.kind == "adape":
                    pe.wait_ge(consts_in, 16 * 11)
                    pe.wait_ge(dve_done, 1)
                    free_turn(s)
                    for k in range(KT):
                        for sect in range(1 + (k >= ON_DVE)):
                            keep_warm(3 if k < ON_DVE else 1)
                            pe.wait_ge(adx_in[2 * k + sect], 16)
                            for j in range(KT):
                                c = 2 * KT * sect + 2 * j
                                ins = pe.matmul(PS[:, b, c:c + 2], ADX[2 * k + sect][:, j * P:j * P + P], SC[:, 0:2, k],
                                                start=k + j + sect == 0, stop=k == KT - 1, skip_group_check=True)
                    ins.then_inc(turn_mm, 1)
                elif s.kind == "adared":
                    free_turn(s)
                    if s.sect == 1:
                        wait_steps(s.after)
                    else:
                        pe.wait_ge(ada_done, KT * (s.sect - 1))
                    for c in range(1 + (s.sect in CTX_SECT)):
                        for j in range(KT):
                            ins = pe.matmul(PS[:, b, c * KT + j:c * KT + j + 1], ACC[:, c, j * P:j * P + P], ONES[:, 0:1],
                                            start=True, stop=True)
                    ins.then_inc(turn_mm, 1)
                elif s.kind == "nstat":
                    if s.g != 0:
                        keep_warm(26 if s.g == 4 else 8)
                    pe.wait_ge(dve_done, s.d0)
                    free_turn(s)
                    for n in range(s.T // P):
                        ins = pe.matmul(PS[:, b, n:n + 1], T4[:, n * P:n * P + P], ONES[:, 0:1], start=True, stop=True)
                    ins.then_inc(turn_mm, 1)
                elif s.kind == "back":
                    keep_warm(2)
                    pe.wait_ge(dve_done, s.d0)
                    free_scores(0, s)
                    for n in range(s.T // P):
                        ins = pe.transpose(SP_[:, 0, n * P:n * P + P], T3[:, n * P:n * P + P], IDN[:])
                    ins.then_inc(score_mm[0], 1)
                elif s.kind == "hnorm":
                    if s.what == "sgv" and s.m:
                        keep_warm(6)
                    wait_steps(s.after)
                    free_scores(0, s)
                    for n in range(s.T // P):
                        ins = pe.matmul(SP_[:, 0, 2 * n:2 * n + 2], T2[:, n * P:n * P + P], BONES[:, 0:P:64], start=True, stop=True)
                    ins.then_inc(score_mm[0], 1)
                elif s.kind == "rope":
                    free_scores(1, s)
                    pe.matmul(SP_[:, 1, 0:TX], PERM[:], T1[:, 0:TX], start=True, stop=True).then_inc(score_mm[1], 1)
                elif s.kind == "vtrans":
                    wait_steps(s.after)
                    free_scores(1, s)
                    for n in range(NT):
                        ins = pe.transpose(SP_[:, 1, n * P:n * P + P], T3[:, n * P:n * P + P], IDN[:])
                    ins.then_inc(score_mm[1], 1)
                elif s.kind == "scores":
                    wait_steps(s.after)
                    free_scores(s.st, s)
                    r = slice(64 * s.half, 64 * s.half + 64)
                    q = slice(s.qt * P, s.qt * P + P)
                    if s.na:
                        qh, ql, kh, kl = (x[r, s.pair % 2] for x in (Qh, Ql, Kh, Kl))
                    else:
                        qh, ql, kh, kl = SQh[r, s.pair], SQl[r, s.pair], SKh[r], SKl[r]
                    for n, (x, y) in enumerate(((qh, kh), (qh, kl), (ql, kh))):
                        if s.nk == NT:
                            for lo, sz in segs(TT):
                                ins = pe.matmul(SP_[:, s.st, lo:lo + sz], x[:, q], y[:, lo:lo + sz], start=n == 0, stop=n == 2)
                        else:
                            ins = pe.matmul(SP_[:, s.st, 0:TC], x[:, q], y[:, TX:TT], start=n == 0, stop=n == 2)
                    ins.then_inc(score_mm[s.st], 1)
                elif s.kind == "trans":
                    wait_steps(s.after)
                    if s.na:
                        free_scores(1, s)
                        dst = SP_[:, 1, :]
                    else:
                        if not s.in_turn:
                            free_turn(s)
                        dst = PS[:, b, :]
                    for n in range(s.nk):
                        c = slice(n * P, n * P + P)
                        if s.na:
                            ins = pe.transpose(dst[:, c], EX[s.eb][:, c], IDN[:])
                        else:
                            ins = pe.matmul(dst[:, c], EX[s.eb][:, c], DIAG[:, s.eb, :], start=True, stop=True)
                    ins.then_inc(score_mm[1] if s.na else turn_mm, 1)
                    if s.idle:
                        keep_warm(6, s.idle)
                elif s.kind == "pvmm":
                    wait_steps(s.after)
                    free_turn(s)
                    k0 = NT - s.nk
                    for n in range(s.nk):
                        for j, (v, p) in enumerate(((Vh, PTh[s.pt]), (Vh, PTl[s.pt]), (Vl, PTh[s.pt]))):
                            ins = pe.matmul(PS[:, b, TT:TT + 256], v[:, k0 + n, :], p[:, n, :], start=n + j == 0,
                                            stop=n == s.nk - 1 and j == 2)
                    if not s.in_turn:
                        ins.then_inc(turn_mm, 1)
                elif s.kind == "gtrans":
                    wait_steps(s.after)
                    free_turn(s)
                    for n in range(s.T // P):
                        ins = pe.transpose(PS[:, b, n * P:n * P + P], GV[:, s.m, n * P:n * P + P], IDN[:])
                    ins.then_inc(turn_mm, 1)
                elif s.kind == "spgate":
                    wait_steps(s.after)
                    free_turn(s)
                    pe.wait_ge(sp_in, 64 * (s.layer + 1))
                    for n in range(s.nn):
                        ins = pe.matmul(PS[:, b, n * 256:n * 256 + 256], GT[s.m][:, s.n0 + n, :], WS[:, s.m * 256:s.m * 256 + 256],
                                        start=True, stop=True)
                    ins.then_inc(turn_mm, 1)
                elif s.kind == "four1":
                    pe.wait_ge(act_done, s.a0)
                    free_turn(s)
                    for n in range(s.nn):
                        c = (s.n0 + n) * P
                        ins = pe.matmul(PS[:, b, n * 256:n * 256 + 256], F[:, s.m, c:c + P], CS[:], start=True, stop=True)
                    ins.then_inc(turn_mm, 1)
                elif s.kind == "four2":
                    wait_steps(s.after)
                    free_turn(s)
                    done_l = sum(x.i < s.i for x in four_first)
                    pe.wait_ge(dft_in, 32 * done_l)
                    for n in range(4):
                        for j, tab in enumerate((DC, DS)):
                            ins = pe.matmul(PS[:, b, 0:TX], AB[:, n, s.m, j * P:j * P + P], tab[:, n, :], start=n + j == 0,
                                            stop=n + j == 4)
                    if s.T == TT:
                        for n in range(2):
                            for j, tab in enumerate((DC, DS)):
                                ins = pe.matmul(PS[:, b, TX:TT], AB[:, 4 + n, s.m, j * P:j * P + P], tab[:, n, 0:TX:2],
                                                start=n + j == 0, stop=n + j == 2)
                    ins.then_inc(turn_mm, 1)

        @block.scalar
        def _(act):
            given, taken, own = [0], [0], [0]

            def give(ins):
                given[0] += 1
                ins.then_inc(for_dve, 1)

            def take():
                taken[0] += 1
                act.wait_ge(for_act, taken[0])

            def chain(ins):
                own[0] += 1
                ins.then_inc(act_own, 1)
                act.wait_ge(act_own, own[0])

            def done(ins):
                ins.then_inc(act_done, 1)

            def load_table(f):
                chain(act.activation(SQT[:], EPSC[:], f))

            def scores_in(b, s):
                act.wait_ge(score_mm[b], s.fill)

            def round_unit(w):
                if w < n_units:
                    act.wait_ge(raw_landed[w % 2], 16 * (w // 2 + 1))
                    if w >= 2:
                        act.wait_ge(turn_mm, turn_of_w[w - 2] + 1)
                    act.activation(Wh[:, w % 2, :], RAW[:, w % 2, :], ACT.Copy).then_inc(w_rounded, 1)

            prev = None
            for s in steps + [None]:
                if prev is not None and prev.kind == "unit" and turn_of_w[prev.w] == prev.turn:
                    round_unit(prev.w + 2)
                if prev is not None and prev.kind == "adape":
                    round_unit(0)
                    round_unit(1)
                prev = s
                if s is None or s.kind in ("upart", "adared", "pool", "spgate", "adape", "scores", "trans", "pvmm", "back", "gnorm", "gain", "adafirst"):
                    continue
                if s.kind == "unit" and (s.ev in DVE_ONLY or (s.ev == "xupd" and not s.nxT)):
                    continue
                if KT - 1 in (s.k if s.kind == "sq0" and s.x0 == 0 else None, s.m if s.kind == "unit" and s.ev == "xupd" else None):
                    load_table(ACT.Sqrt)
                if s.d0 and s.kind != "bias_row":
                    act.wait_ge(dve_done, s.d0)
                if s.a0 and s.kind != "bias_row":
                    act.wait_ge(act_done, s.a0)
                b = None if s.turn is None else s.turn % 2
                ps = None if b is None else PS[:, b, :]
                t = s.T
                if s.turn is not None and not (s.kind == "unit" and s.ev == "xupd"):
                    act.wait_ge(turn_mm, s.turn + 1)
                if s.kind == "silu_c":
                    act.wait_ge(cond_in, 16)
                    give(act.activation(CVT[:], CV[:], ACT.Tanh, scale=0.5))
                elif s.kind == "bias_row":
                    n = s.g * 8 + s.c
                    if n >= 2:
                        act.wait_ge(bias_out[n % 2], 16 * (n // 2))
                    scores_in(s.st, s)
                    act.activation(STAGE[n % 2][0:120, :], SP_[0:120, s.st, 0:512], ACT.Copy).then_inc(rows_done, 1)
                    act.wait_ge(rows_done, s.k)
                    act.dma_start(bias_d[s.g * 120:s.g * 120 + 120, s.c * 8:s.c * 8 + 8, :].rearrange("h c j -> h (c j)"),
                                  STAGE[n % 2][0:120, :]).then_inc(bias_out[n % 2], 16)
                elif s.kind == "sq0":
                    if s.k == 0 and s.x0 == 0:
                        act.wait_ge(x_in, 32)
                    if s.k == 0 and s.x0 == TX:
                        act.wait_ge(ctx2_in, 16)
                    for lo, sz in ([(TX, TC)] if s.x0 else segs(TT)):
                        ins = act.activation(T1[:, lo:lo + sz], xseg(lo, s.k), ACT.Square)
                    give(ins)
                elif s.kind == "nstat":
                    give(act.activation(RMS[:, 0:t // P], ps[:, 0:t // P], ACT.Sqrt, bias=EPSC[:], scale=1.0 / D))
                elif s.kind == "ntile":
                    take()
                    src = (T1, T2)[s.k % 2]
                    for c, (lo, sz) in enumerate(segs(t)):
                        ins = act.activation(Hh[:, s.k, lo:lo + sz], src[:, lo:lo + sz], ACT.Identity,
                                             bias=MOD[:, s.sect, c, s.k:s.k + 1], scale=1.0)
                    give(ins)
                elif s.kind == "final":
                    take()
                    give(act.activation((T1, T2)[s.k % 2][:, 0:t], Xx[:, s.k, :], ACT.Square))
                elif s.kind == "hnorm":
                    scores_in(0, s)
                    n = 2 * t // P
                    give(act.activation(RMS[:, 0:n], SP_[:, 0, 0:n], ACT.Sqrt, bias=EPSC[:], scale=1.0 / 64))
                    if s.what == "sgv":
                        load_table(ACT.Exp if s.m else ACT.Tanh)
                elif s.kind == "rope":
                    scores_in(0, s.back)
                    scores_in(1, s)
                    take()
                    if s.what == "sk":
                        dst = SKh[:, 0:t]
                    else:
                        dst = SQh[:, s.m, 0:t]
                    give(act.activation(dst, T2[:, 0:t], ACT.Copy))
                elif s.kind == "vtrans":
                    scores_in(1, s)
                    give(act.activation(Vh[:], SP_[:, 1, 0:TT].rearrange("p (n f) -> p n f", f=P), ACT.Copy))
                elif s.kind == "soft":
                    x = s.trans
                    if x is not None:
                        if s.na:
                            scores_in(1, x)
                            src = SP_[:, 1, 0:TT]
                        else:
                            act.wait_ge(turn_mm, x.turn + 1)
                            src = PS[:, x.turn % 2, 0:x.nk * P]
                        give(act.activation(PTh[x.pt][:, 0:x.nk, x.col:x.col + P], src.rearrange("p (n q) -> p n q", q=P),
                                            ACT.Copy))
                    x = s.scores
                    if x is not None:
                        st, ex, nk = ST[:, x.qt % 2, :], EX[x.eb], x.nk * P
                        scores_in(x.st, x)
                        take()
                        if s.na:
                            act.activation(ex[:, 0:TX], ex[:, 0:TX], ACT.Exp, bias=st[:, 2:3], scale=1.0, accum_out=st[:, 3:4])
                            give(act.activation(ex[:, TX:TT], SP_[:, 0, TX:TT], ACT.Exp, bias=st[:, 2:3], scale=1.0,
                                                accum_out=st[:, 4:5]))
                        else:
                            give(act.activation(ex[:, 0:nk], SP_[:, x.st, 0:nk], ACT.Exp, bias=st[:, 2:3], scale=1.0,
                                                accum_out=st[:, 3:4]))
                elif s.kind == "pv":
                    r = slice(64 * s.half, 64 * s.half + 64)
                    if s.na:
                        take()
                        give(act.activation(Oh[r, s.tile, s.q0:s.q0 + 256], PVT[r, :], ACT.Copy))
                    else:
                        give(act.activation(Hh[r, s.tile, s.q0:s.q0 + 256], ps[r, TT:TT + 256], ACT.Copy))
                elif s.kind == "gtrans":
                    done(act.activation(GT[s.m][:, 0:t // P, :], ps[:, 0:t].rearrange("p (n f) -> p n f", f=P), ACT.Copy))
                elif s.kind == "gsplit":
                    take()
                    give(act.activation(Hh[:, 6 + s.m, 0:t], (T2, T4)[s.m][:, 0:t], ACT.Copy))
                elif s.kind == "four1":
                    done(act.activation(AB[:, s.n0:s.n0 + s.nn, s.m, :],
                                        ps[:, 0:s.nn * 256].rearrange("p (n f) -> p n f", f=256), ACT.Copy))
                elif s.kind == "four2":
                    for lo, sz in segs(t):
                        ins = act.activation(Hh[:, 4 + s.m, lo:lo + sz], ps[:, lo:lo + sz], ACT.Copy, scale=four_scale(sz))
                    give(ins)
                else:
                    assert s.kind == "unit", s.kind
                    m = s.m
                    if s is first_xupd:
                        for n in range(2):
                            act.wait_ge(bias_out[n], 16 * 8)
                    if s.ev == "u":
                        for lo, sz in segs(t):
                            o = PADL if lo == 0 else UC + PADL
                            ins = act.activation(U[:, o:o + sz], ps[:, lo:lo + sz], ACT.Copy)
                        done(ins)
                    elif s.ev == "g":
                        give(act.activation(G2[:, s.pair % 2, :], ps[:, 0:t], ACT.Tanh, scale=0.5))
                    elif s.ev in ("gate", "cgate"):
                        give(act.activation(T1[:, 0:t], ps[:, 0:t], ACT.Tanh, scale=0.5))
                        if s.ev == "cgate":
                            take()
                            give(act.activation(Oh[:, m, :], T2[:, 0:t], ACT.Copy))
                    elif s.ev == "poolmix":
                        take()
                        give(act.activation(Hh[:, m, 0:t], T2[:, 0:t], ACT.Copy))
                    elif s.ev == "xupd":
                        take()
                        for lo, sz in segs(s.nxT):
                            ins = act.activation(T1[:, lo:lo + sz], xseg(lo, m), ACT.Square)
                        give(ins)
                    elif s.ev in ("q", "k"):
                        dst = (Qh if s.ev == "q" else Kh)[:, s.pair % 2, 0:t]
                        give(act.activation(dst, ps[:, 0:t], ACT.Copy, scale=0.125 if s.ev == "q" else 1.0))
                    elif s.ev in ("v", "cg"):
                        done(act.activation(T3[:, 0:t], ps[:, 0:t], ACT.Copy))
                    elif s.ev in ("sk", "sq"):
                        g = HG[:, s.layer, 1:2] if s.ev == "sk" else HG[:, s.layer, 0:1]
                        act.activation(T1[:, 0:t], ps[:, 0:t], ACT.Copy, scale=g)
                        done(act.activation(T2[:, 0:t], ps[:, 0:t], ACT.Square))
                    elif s.ev == "sf":
                        done(act.activation(F[:, m, 0:t], ps[:, 0:t], ACT.Copy))
                    elif s.ev in ("su", "sgv"):
                        give(act.activation(T1[:, 0:t], ps[:, 0:t], ACT.Square))
                        take()
                        give(act.activation(T1[:, 0:t], T2[:, 0:t], ACT.Tanh, scale=GELU_C))
                        if s.ev == "sgv":
                            load_table(ACT.Sqrt)
                    elif s.ev == "mlp":
                        chain(act.activation(T1[:, 0:t], ps[:, 0:t], ACT.Relu))
                        give(act.activation(Mh[:, m, 0:t], T1[:, 0:t], ACT.Square))

        @block.vector
        def _(dve):
            taken, own = [0], [0]
            chunk = [0]

            def give(ins):
                ins.then_inc(for_act, 1)

            def take():
                taken[0] += 1
                dve.wait_ge(for_dve, taken[0])

            def chain(ins):
                own[0] += 1
                ins.then_inc(dve_own, 1)
                dve.wait_ge(dve_own, own[0])

            def done(ins):
                ins.then_inc(dve_done, 1)

            def scores_in(b, s):
                dve.wait_ge(score_mm[b], s.fill)

            def tt(dst, x, y, op):
                return dve.tensor_tensor(dst, x, y, op)

            def stt(dst, x, c, y, op0, op1):
                return dve.scalar_tensor_tensor(out=dst, in0=x, scalar=c, in1=y, op0=op0, op1=op1)

            def ada_chunk(sect, k):
                n = chunk[0]
                dve.wait_ge(ada_landed[n % 2], 16 * (n // 2 + 1))
                if n:
                    dve.wait_ge(ada_done, n)
                if k == 0:
                    dve.wait_ge(turn_mm, red_turn[sect - 1] + 1)
                base = 0 if sect < 12 else 2
                for c in range(1 + (sect in CTX_SECT)):
                    w = SC[:, base + c, k:k + 1]
                    if k == 0:
                        ins = dve.tensor_scalar(ACC[:, c, :], ADR[:, n % 2, :], w, None, ALU.mult)
                    else:
                        ins = stt(ACC[:, c, :], ADR[:, n % 2, :], w, ACC[:, c, :], ALU.mult, ALU.add)
                ins.then_inc(ada_done, 1)
                chunk[0] += 1

            def normed(s, k):
                dst = (T1, T2)[k % 2]
                for c, (lo, sz) in enumerate(segs(s.T)):
                    ins = stt(dst[:, lo:lo + sz], xseg(lo, k), GA[:, c, k:k + 1], SP_[:, 0, lo:lo + sz], ALU.mult, ALU.mult)
                give(ins)

            def sum_squares(k, parts, sq=T1):
                for lo, sz in parts:
                    if k == 0:
                        ins = dve.tensor_copy(T4[:, lo:lo + sz], sq[:, lo:lo + sz])
                    else:
                        ins = tt(T4[:, lo:lo + sz], T4[:, lo:lo + sz], sq[:, lo:lo + sz], ALU.add)
                return ins

            def window_means(s):
                w = WINDOWS[s.m // 2]
                chain(tt(T1[:, 1:UW], U[:, 0:UW - 1], U[:, 1:UW], ALU.add))
                cur, lo, hi, width = T1, 1, UW, 2
                while width < w:
                    d = width // 2
                    nxt = T2 if cur is T1 else T1
                    lo, hi = lo + d, hi - d
                    chain(tt(nxt[:, lo:hi], cur[:, lo - d:hi - d], cur[:, lo + d:hi + d], ALU.add))
                    cur, width = nxt, width * 2
                parts = [(PADL, 0, TX)] + ([(UC + PADL, TX, TC)] if s.T == TT else [])
                for o, _, sz in parts:
                    for j, q in enumerate((o, o + sz - PADL)):
                        ins = tt(cur[:, q:q + PADL], cur[:, q:q + PADL], EDGE[:, s.m // 2, j, :], ALU.mult)
                chain(ins)
                f = T2 if cur is T1 else T1
                for o, lo, sz in parts:
                    ins = stt(f[:, lo:lo + sz], cur[:, o:o + sz], 1.0 / w, U[:, o:o + sz], ALU.mult, ALU.subtract)
                chain(ins)
                chain(dve.tensor_copy(Dh[:, s.m, 0:s.T], f[:, 0:s.T]))
                done(tt(Dl[:, s.m, 0:s.T], f[:, 0:s.T], Dh[:, s.m, 0:s.T].bitcast(F32), ALU.subtract))

            def rest(lo_dst, src, hi, scale=None):
                if scale is None:
                    return tt(lo_dst, src, hi.bitcast(F32), ALU.subtract)
                return stt(lo_dst, src, scale, hi.bitcast(F32), ALU.mult, ALU.subtract)

            chain(dve.memset(EPSC[:], EPS))
            chain(dve.memset(U[:], 0.0))
            for s in steps:
                b = None if s.turn is None else s.turn % 2
                ps = None if b is None else PS[:, b, :]
                t = s.T
                if ends_in(s) == "dve":
                    if s.a0:
                        dve.wait_ge(act_done, s.a0)
                    if s.d0:
                        dve.wait_ge(dve_done, s.d0)
                    if s.turn is not None:
                        dve.wait_ge(turn_mm, s.turn + 1)
                if s.kind == "silu_c":
                    dve.wait_ge(cond_in, 16)
                    take()
                    chain(stt(CVT[:], CVT[:], 1.0, CV[:], ALU.add, ALU.mult))
                    done(dve.tensor_scalar(SC[:], CVT[:], 0.5, None, ALU.mult))
                elif s.kind == "adafirst":
                    for k in range(ON_DVE):
                        dve.wait_ge(adx_in[2 * k + 1], 16)
                        for c in range(2):
                            w = SC[:, c, k:k + 1]
                            if k == 0:
                                ins = dve.tensor_scalar(ACC[:, c, :], ADX[1], w, None, ALU.mult)
                            else:
                                if c == 0:
                                    chain(ins)
                                ins = stt(ACC[:, c, :], ADX[2 * k + 1], w, ACC[:, c, :], ALU.mult, ALU.add)
                    done(ins)
                elif s.kind == "gain":
                    if s.g == 0:
                        dve.tensor_scalar(PSC[:], PSC[:], 0.5, None, ALU.mult)
                        dve.tensor_scalar(HG[:, :, 2:4], HG[:, :, 2:4], 0.5, None, ALU.mult)
                    if s.g == 3:
                        dve.memset(U[:], 0.0)
                    for c in range(1 + (t == TT)):
                        ins = stt(GA[:, c, :], MOD[:, s.sect + 1, c, :], 1.0, NG[:, s.g, :], ALU.add, ALU.mult)
                    done(ins)
                elif s.kind == "adape":
                    dve.wait_ge(consts_in, 16 * 11)
                    for sect in range(2):
                        for c in range(2):
                            c0 = 2 * KT * sect + c
                            ins = tt(MOD[:, sect, c, :], ps[:, c0:c0 + 2 * KT - 1:2], ADAB[:, sect, :], ALU.add)
                    done(ins)
                elif s.kind == "adared":
                    n = 1 + (s.sect in CTX_SECT)
                    for c in range(n):
                        rest_of = MOD[:, 1, c, :] if s.sect == 1 else ADAB[:, s.sect, :]
                        ins = tt(MOD[:, s.sect, c, :], ps[:, c * KT:c * KT + KT], rest_of, ALU.add)
                    done(ins)
                elif s.kind == "sq0":
                    take()
                    done(sum_squares(s.k, [(TX, TC)] if s.x0 else segs(TT)))
                elif s.kind == "nstat":
                    take()
                    n = t // P
                    chain(dve.reciprocal(RMS[:, 0:n], RMS[:, 0:n]))
                    done(dve.tensor_copy(T3[:, 0:t].rearrange("p (n f) -> p n f", f=P),
                                         RMS[:, 0:n].unsqueeze(2).broadcast_to((P, n, P))))
                elif s.kind == "ntile":
                    if s.k == 0:
                        scores_in(0, s.back)
                        normed(s, 0)
                    if s.k < KT - 1:
                        normed(s, s.k + 1)
                    take()
                    src = (T1, T2)[s.k % 2]
                    for c, (lo, sz) in enumerate(segs(t)):
                        ins = stt(Hl[:, s.k, lo:lo + sz], src[:, lo:lo + sz], MOD[:, s.sect, c, s.k:s.k + 1],
                                  Hh[:, s.k, lo:lo + sz].bitcast(F32), ALU.add, ALU.subtract)
                    done(ins)
                elif s.kind == "final":
                    if s.k == 0:
                        scores_in(0, s.back)
                    for k in ([0, 1] if s.k == 0 else [s.k + 1] if s.k < KT - 1 else []):
                        give(stt(Xx[:, k, :], Xx[:, k, :], NG[:, 8, k:k + 1], SP_[:, 0, 0:t], ALU.mult, ALU.mult))
                    take()
                    done(sum_squares(s.k, segs(TX), (T1, T2)[s.k % 2]))
                elif s.kind == "pool":
                    window_means(s)
                elif s.kind == "hnorm":
                    scores_in(0, s)
                    take()
                    n = 2 * t // P
                    chain(dve.reciprocal(RMS[:, 0:n], RMS[:, 0:n]))
                    done(dve.tensor_copy(T3[:, 0:t].rearrange("p (n f) -> p n f", f=64),
                                         RMS[:, 0:n].unsqueeze(2).broadcast_to((P, n, 64))))
                elif s.kind == "gnorm":
                    scores_in(0, s.back)
                    done(stt(GV[:, s.m, 0:t], GV[:, s.m, 0:t], HG[:, s.layer, 2 + s.m:3 + s.m], SP_[:, 0, 0:t],
                             ALU.mult, ALU.mult))
                elif s.kind == "rope":
                    scores_in(0, s.back)
                    scores_in(1, s)
                    if s.what == "sk":
                        dve.wait_ge(sp_in, 64 * (s.layer + 1))
                    tt(T4[:, 0:TX], T1[:, 0:TX], ROPC[:], ALU.mult)
                    chain(tt(T2[:, 0:TX], SP_[:, 1, 0:TX], ROPS[:], ALU.mult))
                    chain(tt(T4[:, 0:TX], T4[:, 0:TX], T2[:, 0:TX], ALU.add))
                    c = 1.0 if s.what == "sk" else 0.125
                    ins = stt(T2[:, 0:TX], T4[:, 0:TX], c, SP_[:, 0, 0:TX], ALU.mult, ALU.mult)
                    if t == TT:
                        ins = stt(T2[:, TX:TT], T1[:, TX:TT], c, SP_[:, 0, TX:TT], ALU.mult, ALU.mult)
                    give(ins)
                    take()
                    hi, lo = (SKh[:, 0:t], SKl[:, 0:t]) if s.what == "sk" else (SQh[:, s.m, 0:t], SQl[:, s.m, 0:t])
                    done(rest(lo, T2[:, 0:t], hi))
                elif s.kind == "vtrans":
                    scores_in(1, s)
                    take()
                    done(rest(Vl[:], SP_[:, 1, 0:TT].rearrange("p (n f) -> p n f", f=P), Vh[:]))
                elif s.kind == "soft":
                    x = s.scores
                    if x is not None:
                        st, ex, nk = ST[:, x.qt % 2, :], EX[x.eb], x.nk * P
                        scores_in(x.st, x)
                        if s.na:
                            if x.first:
                                h = x.pair * 2 + x.half
                                dve.wait_ge(bias_in[h % 2], 32 * (h // 2 + 1))
                            bias = BIAS[(x.pair * 2 + x.half) % 2][:, (6 - 2 * x.qt) * 64:(14 - 2 * x.qt) * 64]
                            dve.tensor_tensor_reduce(ex[:, 0:TX], SP_[:, 0, 0:TX], bias, 1.0, -3.0e38, ALU.add, ALU.max,
                                                     st[:, 0:1])
                            chain(dve.tensor_reduce(st[:, 1:2], SP_[:, 0, TX:TT], AX.X, ALU.max))
                            give(dve.tensor_scalar(st[:, 2:3], st[:, 0:1], st[:, 1:2], -1.0, ALU.max, ALU.mult))
                        else:
                            give(dve.tensor_reduce(st[:, 2:3], SP_[:, x.st, 0:nk], AX.X, ALU.max, negate=True))
                    y = s.trans
                    if y is not None:
                        if s.na:
                            scores_in(1, y)
                            src = SP_[:, 1, 0:TT]
                        else:
                            dve.wait_ge(turn_mm, y.turn + 1)
                            src = PS[:, y.turn % 2, 0:y.nk * P]
                        take()
                        ins = rest(PTl[y.pt][:, 0:y.nk, y.col:y.col + P], src.rearrange("p (n q) -> p n q", q=P),
                                   PTh[y.pt][:, 0:y.nk, y.col:y.col + P])
                    if x is not None:
                        take()
                        if s.na:
                            chain(tt(st[:, 5:6], st[:, 3:4], st[:, 4:5], ALU.add))
                            chain(dve.reciprocal(st[:, 6:7], st[:, 5:6]))
                        else:
                            chain(dve.reciprocal(st[:, 6:7], st[:, 3:4]))
                        if s.na:
                            ins = dve.tensor_scalar(ex[:, 0:nk], ex[:, 0:nk], st[:, 6:7], None, ALU.mult)
                        else:
                            ins = dve.tensor_scalar(DIAG[:, x.eb, :], IDN[:], st[:, 6:7], None, ALU.mult)
                    done(ins)
                elif s.kind == "pv":
                    r = slice(64 * s.half, 64 * s.half + 64)
                    q = slice(s.q0, s.q0 + 256)
                    if s.na:
                        give(stt(PVT[r, :], ps[r, TT:TT + 256], 0.5, G2[r, s.pair % 2, q], ALU.mult, ALU.mult))
                        take()
                        done(rest(Ol[r, s.tile, q], PVT[r, :], Oh[r, s.tile, q]))
                    else:
                        take()
                        done(rest(Hl[r, s.tile, q], ps[r, TT:TT + 256], Hh[r, s.tile, q]))
                elif s.kind == "spgate":
                    for n in range(s.nn):
                        for h in range(2):
                            r = slice(64 * h, 64 * h + 64)
                            c = (s.n0 + n) * P
                            ins = tt((T2, T4)[s.m][r, c:c + P], ps[r, n * 256 + h * P:n * 256 + h * P + P], BS[r, s.m, :], ALU.add)
                    done(ins)
                elif s.kind == "gsplit":
                    z = (T2, T4)[s.m]
                    give(stt(z[:, 0:t], z[:, 0:t], 0.5, SU[:, s.m, 0:t], ALU.mult, ALU.mult))
                    take()
                    done(rest(Hl[:, 6 + s.m, 0:t], z[:, 0:t], Hh[:, 6 + s.m, 0:t]))
                elif s.kind == "four2":
                    take()
                    for lo, sz in segs(t):
                        ins = rest(Hl[:, 4 + s.m, lo:lo + sz], ps[:, lo:lo + sz], Hh[:, 4 + s.m, lo:lo + sz], four_scale(sz))
                    done(ins)
                elif s.kind == "unit":
                    m = s.m
                    if s.ev == "gate":
                        take()
                        done(stt(G[:, m, 0:t], T1[:, 0:t], 1.0, ps[:, 0:t], ALU.add, ALU.mult))
                    elif s.ev == "g":
                        take()
                        done(stt(G2[:, s.pair % 2, :], G2[:, s.pair % 2, :], 1.0, ps[:, 0:t], ALU.add, ALU.mult))
                    elif s.ev == "cgate":
                        take()
                        chain(stt(T2[:, 0:t], T1[:, 0:t], 1.0, ps[:, 0:t], ALU.add, ALU.mult))
                        give(tt(T2[:, 0:t], T2[:, 0:t], T4[:, 0:t], ALU.mult))
                        take()
                        done(rest(Ol[:, m, :], T2[:, 0:t], Oh[:, m, :]))
                    elif s.ev == "poolmix":
                        give(stt(T2[:, 0:t], ps[:, 0:t], PSC[:, s.layer, m:m + 1], G[:, m, 0:t], ALU.mult, ALU.mult))
                        take()
                        done(rest(Hl[:, m, 0:t], T2[:, 0:t], Hh[:, m, 0:t]))
                    elif s.ev == "xupd":
                        for c, (lo, sz) in enumerate(segs(t)):
                            ins = stt(xseg(lo, m), ps[:, lo:lo + sz], MOD[:, s.sect, c, m:m + 1], xseg(lo, m), ALU.mult, ALU.add)
                        if s.nxT:
                            give(ins)
                            take()
                            ins = sum_squares(m, segs(s.nxT))
                        done(ins)
                    elif s.ev in ("q", "k"):
                        take()
                        hi, lo = (Qh, Ql) if s.ev == "q" else (Kh, Kl)
                        p = s.pair % 2
                        done(rest(lo[:, p, 0:t], ps[:, 0:t], hi[:, p, 0:t], 0.125 if s.ev == "q" else None))
                    elif s.ev == "cv":
                        if m == 0:
                            dve.memset(Z[:, 0:TX + 2:TX + 1], 0.0)
                        chain(tt(Z[:, 1:TX + 1], ps[:, 0:TX], T3[:, 0:TX], ALU.mult))
                        chain(dve.tensor_scalar(T4[:, 0:TX], Z[:, 0:TX], CW[:, 0, m:m + 1], CW[:, 3, m:m + 1], ALU.mult, ALU.add))
                        chain(stt(T4[:, 0:TX], Z[:, 1:TX + 1], CW[:, 1, m:m + 1], T4[:, 0:TX], ALU.mult, ALU.add))
                        done(stt(T4[:, 0:TX], Z[:, 2:TX + 2], CW[:, 2, m:m + 1], T4[:, 0:TX], ALU.mult, ALU.add))
                    elif s.ev == "cb":
                        done(stt(T4[:, 0:TX], ps[:, 0:TX], 0.5, T4[:, 0:TX], ALU.mult, ALU.mult))
                    elif s.ev in ("su", "sgv"):
                        take()
                        chain(dve.tensor_scalar(T2[:, 0:t], T1[:, 0:t], GELU_A, 1.0, ALU.mult, ALU.add))
                        give(tt(T2[:, 0:t], T2[:, 0:t], ps[:, 0:t], ALU.mult))
                        take()
                        if s.ev == "su":
                            done(stt(SU[:, m, 0:t], T1[:, 0:t], 1.0, ps[:, 0:t], ALU.add, ALU.mult))
                        else:
                            chain(stt(GV[:, m, 0:t], T1[:, 0:t], 1.0, ps[:, 0:t], ALU.add, ALU.mult))
                            done(stt(T2[:, 0:t], GV[:, m, 0:t], 0.25, GV[:, m, 0:t], ALU.mult, ALU.mult))
                    elif s.ev == "mlp":
                        take()
                        chain(tt(T2[:, 0:t], T1[:, 0:t], T1[:, 0:t], ALU.mult))
                        done(rest(Ml[:, m, 0:t], T2[:, 0:t], Mh[:, m, 0:t]))
                if s.ada and s.d1:
                    dve.wait_ge(dve_done, s.d1)
                for sect, k in s.ada:
                    ada_chunk(sect, k)


def four_scale(n):
    return float(1.0 / np.sqrt(n * 64.0))


def unit_columns(w, cols):
    return np.ascontiguousarray(w[:, cols].reshape(-1, P, len(cols)).transpose(1, 0, 2)).reshape(P, -1)


def constants():
    c = {}
    eye = np.eye(P, dtype=np.float32)
    c["ident"], c["ones"] = eye, np.ones((P, P), np.float32)
    c["bones"] = np.kron(np.eye(2), np.ones((64, 64))).astype(np.float32)
    swap = np.arange(P) ^ 16
    c["perm"] = eye[swap]
    hot = np.zeros((32, GRID_W, GRID_W), np.float32)
    for q in range(GRID_W):
        first = min(max(q - WIN // 2, 0), GRID_W - WIN)
        for j in range(GRID_W):
            if first <= j < first + WIN:
                hot[j - q + WIN - 1, q, j] = 1.0
            else:
                hot[NDC, q, j] = MASKED
    hot = np.concatenate([hot.reshape(32, -1), np.zeros((32, 512), np.float32)], 1)
    c["onehot"] = hot.reshape(32, 3, 1536).transpose(1, 0, 2).reshape(96, 1536)
    n = np.arange(64)
    a = 2 * np.pi * ((n[:, None] * n) % 64) / 64
    c["dft64"] = np.concatenate([np.kron(np.eye(2), np.cos(a)), np.kron(np.eye(2), np.sin(a))], 1).astype(np.float32)
    n = np.arange(TX)
    a = 2 * np.pi * ((n[:, None] * n) % TX) / TX
    c["dft_cos"] = np.cos(a).reshape(4, P, TX).transpose(1, 0, 2).astype(np.float32)
    c["dft_sin"] = (-np.sin(a)).reshape(4, P, TX).transpose(1, 0, 2).astype(np.float32)
    edge = np.zeros((P, 4, 2, PADL), np.float32)
    for g, w in enumerate(WINDOWS):
        for j in range(PADL):
            for side, (i, size) in enumerate(((j, TX), (TX - PADL + j, TX))):
                edge[:, g, side, j] = w / (min(i + w // 2, size) - max(i - w // 2, 0))
    c["edge"] = edge
    inv = np.float32(10000.0) ** (-np.arange(0, 32, 2, dtype=np.float32) / np.float32(32))
    tok = np.arange(TX)
    cos, sin = np.zeros((P, TX), np.float32), np.zeros((P, TX), np.float32)
    for p in range(P):
        f = p % 64
        pos = (tok // GRID_W if f < 32 else tok % GRID_W).astype(np.float32)
        ang = (pos * inv[f % 16]).astype(np.float32)
        cos[p] = np.cos(ang)
        sin[p] = np.sin(ang) * (-1 if f % 32 < 16 else 1)
    c["rope_cos"], c["rope_sin"] = cos, sin
    return c


def layout(i):
    i = {k: np.asarray(v) for k, v in i.items()}
    a = constants()
    a["xT"] = np.ascontiguousarray(i["x"][0].T)
    a["ctxT"] = np.ascontiguousarray(i["ctx"][0].T)
    a["ctxT_2"] = np.ascontiguousarray(i["ctx_2"][0].T)
    col = lambda v: np.ascontiguousarray(np.asarray(v).reshape(-1, P).T)
    a["cond"] = np.stack([col(i["c"][0]), col(i["c_ctx"]), col(i["c_2"][0]), col(i["c_ctx_2"])], 1)
    units = []

    def cols(w, m0, n=P):
        units.append(unit_columns(w, np.arange(m0, m0 + n)))

    def pool_units(j):
        for m in range(16):
            cols(i["pool_w_in"][j], m * P)
        grp = i["pool_w_grp"][j]
        for half in range(2):
            units.append(np.concatenate([unit_columns(grp[m // 2], np.arange(m % 2 * P, m % 2 * P + P))
                                         for m in range(half * 4, half * 4 + 4)], 1))
        for m in range(8):
            cols(i["pool_w_out"][j], m * P)

    pool_units(0)
    w = i["na_w_in"][0]
    for t in range(8):
        for part in (0, 1, 3, 2):
            cols(w, part * D + t * P)
    for m in range(8):
        cols(i["na_w_out"][0], m * P)
    w = i["conv_w_in"][0]
    for t in range(8):
        for part in (1, 2, 0, 3):
            cols(w, part * D + t * P)
    for m in range(8):
        cols(i["conv_w_out"][0], m * P)
    pool_units(1)
    for L in range(2):
        w = i["w_in_2"][L]
        cols(w, 512)
        pairs = [np.concatenate([np.arange(m * 64, m * 64 + 64), np.arange((m + 4) * 64, (m + 4) * 64 + 64)]) for m in range(4)]
        for m in range(4):
            units.append(unit_columns(w, pairs[m]))
        cols(w, 640)
        for m in range(6):
            cols(w, 768 + m * P)
        wo = i["w_out_2"][L][np.concatenate(pairs + [np.arange(512, 1024)])]
        for m in range(8):
            cols(wo, m * P)
        for c in range(4):
            for m in range(8):
                cols(i["w_mlp1_2"][L], c * D + m * P)
            for m in range(8):
                cols(i["w_mlp2_2"][L][c * D:c * D + D], m * P)
    a["wpack"] = np.stack(units)
    ada = [i["ada_w"][L][:, s * D:s * D + D] for L in range(4) for s in range(3)]
    ada += [i["w_ada_2"][L][:, s * D:s * D + D] for L in range(2) for s in range(6)]
    a["adapack"] = np.concatenate([x.reshape(8, P, D) for x in ada])
    bias = [i["ada_b"][L][s * D:s * D + D] for L in range(4) for s in range(3)]
    bias += [i["b_ada_2"][L][s * D:s * D + D] for L in range(2) for s in range(6)]
    a["adab"] = np.stack([col(x) for x in bias], 1)
    gains = [*i["norm_g"], *i["norm1_g_2"], *i["norm2_g_2"], i["final_g"]]
    a["normg"] = np.stack([col(x) for x in gains], 1)
    a["psc"] = np.stack([col(x) for x in i["pool_scale"]], 1)
    a["cw"] = np.stack([col(x) for x in [*i["conv_dw"][0], i["conv_db"][0]]], 1)
    twice = lambda v: np.concatenate([v, v])
    a["hg"] = np.stack([np.stack([twice(i["q_norm_g_2"][L]), twice(i["k_norm_g_2"][L]), i["gmlp_v_g_2"][L][:P],
                                  i["gmlp_v_g_2"][L][P:]], 1) for L in range(2)], 1)
    rpb = np.ones((32, 240), np.float32)
    rpb[:NDC] = i["na_rpb"][0].reshape(240, NDC).T
    a["rpb"] = np.concatenate([rpb] * 3)
    a["wsp"] = np.ascontiguousarray(i["w_spatial_2"].transpose(0, 3, 1, 2)).reshape(2, P, 512)
    bs = i["b_spatial_2"].reshape(2, 2, 2, 1, P)
    a["bsp"] = np.ascontiguousarray(np.broadcast_to(bs, (2, 2, 2, 64, P)).transpose(0, 2, 3, 1, 4)).reshape(2, P, 2, P)
    return {k: np.ascontiguousarray(v) for k, v in a.items()}


def kernel(**inputs):
    import concourse.bacc as bacc
    from concourse.bass_utils import run_bass_kernel_spmd

    arrays = layout(inputs)
    nc = bacc.Bacc("TRN2", target_bir_lowering=False, num_devices=1)
    aps = {k: nc.dram_tensor("in_" + k, v.shape, mybir.dt.from_np(v.dtype), kind="ExternalInput").ap()
           for k, v in arrays.items()}
    out = nc.dram_tensor("out_xT", (D, TX), F32, kind="ExternalOutput").ap()
    build_blocks(nc, aps, out)
    r = run_bass_kernel_spmd(nc, [{"in_" + k: v for k, v in arrays.items()}], core_ids=[0])
    return r.results[0]["out_xT"].T[None]
```
